# Optimizing a Trainium2 kernel written in Bass

```python
import math
import numpy as np
import jax
import jax.numpy as jnp
from jax import lax

D_MODEL = 1024
BATCH = 1
SEQ = 1024
DEPTH = 1

NORM_EPS = 1e-6
GLA_HEADS = 4
GLA_DV = D_MODEL // GLA_HEADS
GLA_DK = GLA_DV // 2
GLA_QK = GLA_HEADS * GLA_DK
GLA_GATE_RANK = 16
GLA_GATE_NORM = 16.0
GLA_CHUNK = 16
MLSTM_HEADS = 4
MLSTM_DV = D_MODEL // MLSTM_HEADS
MLSTM_DK = MLSTM_DV // 2
MLSTM_QK = MLSTM_HEADS * MLSTM_DK
MLSTM_CHUNK = 64
MLSTM_GATE_CAP = 15.0
MLSTM_M_INIT = -1e30
GDN_HEADS = 8
GDN_DK = D_MODEL // GDN_HEADS
GDN_DV = D_MODEL // GDN_HEADS
GDN_QKV = GDN_HEADS * (2 * GDN_DK + GDN_DV)
GDN_CONV = 4
GDN_CHUNK = 64
N_BRANCHES = 3
D_FF = ((8 * D_MODEL + 3 * 256 - 1) // (3 * 256)) * 256
IN_SIZES = (GLA_QK, GLA_QK, D_MODEL, D_MODEL, GLA_GATE_RANK,
            MLSTM_QK, MLSTM_QK, D_MODEL, D_MODEL, MLSTM_HEADS, MLSTM_HEADS,
            GDN_QKV, D_MODEL, GDN_HEADS, GDN_HEADS,
            N_BRANCHES * D_MODEL)
D_IN = sum(IN_SIZES)

kernel_name = 'hybrid_gla_mlstm_gdn_adaln_block'

def rmsnorm(x, gain):
    xf = x.astype(jnp.float32)
    y = xf * lax.rsqrt(jnp.mean(xf * xf, axis=-1, keepdims=True) + NORM_EPS)
    return (y * gain.astype(jnp.float32)).astype(x.dtype)

def to_chunks(t, n_heads, head_dim, chunk):
    b, s = t.shape[0], t.shape[1]
    t = t.reshape(b, s // chunk, chunk, n_heads, head_dim)
    return t.transpose(0, 3, 1, 2, 4).astype(jnp.float32)

def gate_chunks(t, chunk):
    b, s, h = t.shape
    return t.reshape(b, s // chunk, chunk, h).transpose(0, 3, 1, 2).astype(jnp.float32)

def from_chunks(o):
    b, h, n, c, d = o.shape
    return o.transpose(0, 2, 3, 1, 4).reshape(b, n * c, h, d)

def chunk_major(*ts):
    return tuple(jnp.moveaxis(t, 2, 0) for t in ts)

def causal_mask(c, strict=False):
    return jnp.tril(jnp.ones((c, c), dtype=bool), -1 if strict else 0)

def softcap(t, cap):
    return cap * jnp.tanh(t / cap)

def l2norm(t):
    return t * lax.rsqrt(jnp.sum(t * t, axis=-1, keepdims=True) + NORM_EPS)

def causal_depthwise_conv(t, w):
    return lax.conv_general_dilated(
        t, w[:, None, :], window_strides=(1,), padding=[(w.shape[0] - 1, 0)],
        dimension_numbers=('NWC', 'WIO', 'NWC'), feature_group_count=t.shape[-1])

def gla_mixer(q, k, v, r, g_lr, w_g2, b_g2, norm_gain):
    b, s, _ = q.shape
    f32 = jnp.float32
    log_alpha = jax.nn.log_sigmoid(g_lr.astype(f32) @ w_g2.astype(f32) + b_g2.astype(f32)) / GLA_GATE_NORM
    qc = to_chunks(q, GLA_HEADS, GLA_DK, GLA_CHUNK) * (GLA_DK ** -0.5)
    kc = to_chunks(k, GLA_HEADS, GLA_DK, GLA_CHUNK)
    vc = to_chunks(v, GLA_HEADS, GLA_DV, GLA_CHUNK)
    cum = jnp.cumsum(to_chunks(log_alpha, GLA_HEADS, GLA_DK, GLA_CHUNK), axis=3)
    q_dec = qc * jnp.exp(cum)
    k_inv = kc * jnp.exp(-cum)
    k_end = kc * jnp.exp(cum[..., -1:, :] - cum)
    decay_last = jnp.exp(cum[..., -1, :])
    scores = jnp.einsum('bhntd,bhnsd->bhnts', q_dec, k_inv)
    scores = jnp.where(causal_mask(GLA_CHUNK), scores, 0.0)
    o_intra = jnp.einsum('bhnts,bhnsv->bhntv', scores, vc)

    def step(state, inp):
        qd, ke, vv, dl = inp
        o = jnp.einsum('bhtk,bhkv->bhtv', qd, state)
        state = state * dl[..., None] + jnp.einsum('bhsk,bhsv->bhkv', ke, vv)
        return state, o

    s0 = jnp.zeros((b, GLA_HEADS, GLA_DK, GLA_DV), f32)
    _, o_inter = lax.scan(step, s0, chunk_major(q_dec, k_end, vc, decay_last))
    o = o_intra + jnp.moveaxis(o_inter, 0, 2)
    o = rmsnorm(from_chunks(o), norm_gain).reshape(b, s, D_MODEL)
    return o * jax.nn.silu(r.astype(f32))

def mlstm_mixer(q, k, v, o_raw, i_raw, f_raw, i_bias, f_bias, norm_gain):
    b, s, _ = q.shape
    f32 = jnp.float32
    c = MLSTM_CHUNK
    qc = to_chunks(q, MLSTM_HEADS, MLSTM_DK, c) * (MLSTM_DK ** -0.5)
    kc = to_chunks(k, MLSTM_HEADS, MLSTM_DK, c)
    vc = to_chunks(v, MLSTM_HEADS, MLSTM_DV, c)
    log_i = gate_chunks(softcap(i_raw.astype(f32) + i_bias.astype(f32), MLSTM_GATE_CAP), c)
    log_f = jax.nn.log_sigmoid(gate_chunks(softcap(f_raw.astype(f32) + f_bias.astype(f32), MLSTM_GATE_CAP), c))
    cum = jnp.cumsum(log_f, axis=-1)
    log_d = cum[..., :, None] - cum[..., None, :] + log_i[..., None, :]
    log_d = jnp.where(causal_mask(c), log_d, -jnp.inf)
    m_intra = jnp.max(log_d, axis=-1)
    sc = jnp.einsum('bhntd,bhnsd->bhnts', qc, kc) * jnp.exp(log_d - m_intra[..., None])
    num_intra = jnp.einsum('bhnts,bhnsv->bhntv', sc, vc)
    den_intra = jnp.sum(sc, axis=-1)
    log_end = cum[..., -1:] - cum + log_i
    m_end = jnp.max(log_end, axis=-1)
    cum_last = cum[..., -1]

    def step(carry, inp):
        cs, ns, m = carry
        qq, kk, vv, cm, mi, numi, deni, le, me, cl = inp
        m_inter = cm + m[..., None]
        m_t = jnp.maximum(m_inter, mi)
        a_inter = jnp.exp(m_inter - m_t)
        a_intra = jnp.exp(mi - m_t)
        num = a_intra[..., None] * numi + a_inter[..., None] * jnp.einsum('bhtk,bhkv->bhtv', qq, cs)
        den = a_intra * deni + a_inter * jnp.einsum('bhtk,bhk->bht', qq, ns)
        h = num / jnp.maximum(jnp.abs(den), jnp.exp(-m_t))[..., None]
        m_new = jnp.maximum(cl + m, me)
        w = jnp.exp(le - m_new[..., None])
        dec = jnp.exp(cl + m - m_new)
        kw = kk * w[..., None]
        cs = dec[..., None, None] * cs + jnp.einsum('bhsk,bhsv->bhkv', kw, vv)
        ns = dec[..., None] * ns + jnp.sum(kw, axis=2)
        return (cs, ns, m_new), h

    init = (jnp.zeros((b, MLSTM_HEADS, MLSTM_DK, MLSTM_DV), f32),
            jnp.zeros((b, MLSTM_HEADS, MLSTM_DK), f32),
            jnp.full((b, MLSTM_HEADS), MLSTM_M_INIT, f32))
    xs = chunk_major(qc, kc, vc, cum, m_intra, num_intra, den_intra, log_end, m_end, cum_last)
    _, h = lax.scan(step, init, xs)
    h = rmsnorm(from_chunks(jnp.moveaxis(h, 0, 2)), norm_gain).reshape(b, s, D_MODEL)
    return h * jax.nn.sigmoid(o_raw.astype(f32))

def gdn_mixer(qkv_raw, z, a_raw, b_raw, conv_w, a_log, dt_bias, norm_gain):
    b, s, _ = qkv_raw.shape
    f32 = jnp.float32
    c = GDN_CHUNK
    qkv = jax.nn.silu(causal_depthwise_conv(qkv_raw.astype(f32), conv_w.astype(f32)))
    q, k, v = jnp.split(qkv, [GDN_HEADS * GDN_DK, 2 * GDN_HEADS * GDN_DK], axis=-1)
    qc = l2norm(to_chunks(q, GDN_HEADS, GDN_DK, c)) * (GDN_DK ** -0.5)
    kc = l2norm(to_chunks(k, GDN_HEADS, GDN_DK, c))
    vc = to_chunks(v, GDN_HEADS, GDN_DV, c)
    beta = gate_chunks(jax.nn.sigmoid(b_raw.astype(f32)), c)
    g = -jnp.exp(a_log.astype(f32)) * jax.nn.softplus(a_raw.astype(f32) + dt_bias.astype(f32))
    cum = jnp.cumsum(gate_chunks(g, c), axis=-1)
    gamma = jnp.exp(jnp.where(causal_mask(c), cum[..., :, None] - cum[..., None, :], -jnp.inf))
    kk = jnp.einsum('bhnid,bhnjd->bhnij', kc, kc)
    a_mat = jnp.where(causal_mask(c, strict=True), beta[..., :, None] * kk * gamma, 0.0)
    t_mat = a_mat + jnp.eye(c, dtype=f32)
    u = lax.linalg.triangular_solve(t_mat, vc * beta[..., None], left_side=True, lower=True, unit_diagonal=True)
    w = lax.linalg.triangular_solve(t_mat, kc * (beta * jnp.exp(cum))[..., None], left_side=True, lower=True, unit_diagonal=True)
    a_qk = jnp.einsum('bhnid,bhnjd->bhnij', qc, kc) * gamma
    q_dec = qc * jnp.exp(cum)[..., None]
    k_end = kc * jnp.exp(cum[..., -1:] - cum)[..., None]
    decay_last = jnp.exp(cum[..., -1])

    def step(state, inp):
        qd, ke, ww, uu, aq, dl = inp
        v_new = uu - jnp.einsum('bhck,bhkv->bhcv', ww, state)
        o = jnp.einsum('bhck,bhkv->bhcv', qd, state) + jnp.einsum('bhts,bhsv->bhtv', aq, v_new)
        state = state * dl[..., None, None] + jnp.einsum('bhsk,bhsv->bhkv', ke, v_new)
        return state, o

    s0 = jnp.zeros((b, GDN_HEADS, GDN_DK, GDN_DV), f32)
    _, o = lax.scan(step, s0, chunk_major(q_dec, k_end, w, u, a_qk, decay_last))
    o = rmsnorm(from_chunks(jnp.moveaxis(o, 0, 2)), norm_gain)
    o = o * jax.nn.silu(z.astype(f32).reshape(b, s, GDN_HEADS, GDN_DV))
    return o.reshape(b, s, D_MODEL)

def hybrid_mixer(h, w_in, gla_w_g2, gla_b_g2, gla_norm, ml_i_bias, ml_f_bias, ml_norm,
                 gdn_conv, gdn_a_log, gdn_dt_bias, gdn_norm, w_out):
    b, s, _ = h.shape
    proj = h @ w_in
    offsets = [int(o) for o in np.cumsum(IN_SIZES)[:-1]]
    (gla_q, gla_k, gla_v, gla_r, gla_glr,
     ml_q, ml_k, ml_v, ml_o, ml_i, ml_f,
     gdn_qkv, gdn_z, gdn_a, gdn_b, merge) = jnp.split(proj, offsets, axis=-1)
    y_gla = gla_mixer(gla_q, gla_k, gla_v, gla_r, gla_glr, gla_w_g2, gla_b_g2, gla_norm)
    y_ml = mlstm_mixer(ml_q, ml_k, ml_v, ml_o, ml_i, ml_f, ml_i_bias, ml_f_bias, ml_norm)
    y_gdn = gdn_mixer(gdn_qkv, gdn_z, gdn_a, gdn_b, gdn_conv, gdn_a_log, gdn_dt_bias, gdn_norm)
    gates = jax.nn.sigmoid(merge.astype(jnp.float32)).reshape(b, s, N_BRANCHES, D_MODEL)
    y = gates[:, :, 0] * y_gla + gates[:, :, 1] * y_ml + gates[:, :, 2] * y_gdn
    return (y @ w_out.astype(jnp.float32)).astype(h.dtype)

def swiglu(h, w_up, w_down):
    gate, val = jnp.split(h @ w_up, 2, axis=-1)
    return (jax.nn.silu(gate) * val) @ w_down

def setup_inputs(seed: int = 0) -> dict:
    key = jax.random.key(seed)
    ks = jax.random.split(key, 24)
    f32 = jnp.float32
    L = DEPTH

    def nrm(k, shape, scale):
        return jax.random.normal(k, shape, f32) * scale

    dt = jnp.exp(jax.random.uniform(ks[15], (L, GDN_HEADS), f32, math.log(1e-3), math.log(0.1)))
    return {
        'x': nrm(ks[0], (BATCH, SEQ, D_MODEL), 1.0),
        'c': nrm(ks[1], (BATCH, D_MODEL), 1.0),
        'ada_w': nrm(ks[2], (L, D_MODEL, 6 * D_MODEL), 0.5 * D_MODEL ** -0.5),
        'ada_b': nrm(ks[3], (L, 6 * D_MODEL), 0.02),
        'norm_mix': 1.0 + nrm(ks[4], (L, D_MODEL), 0.05),
        'norm_ffn': 1.0 + nrm(ks[5], (L, D_MODEL), 0.05),
        'w_in': nrm(ks[6], (L, D_MODEL, D_IN), D_MODEL ** -0.5),
        'gla_w_g2': nrm(ks[7], (L, GLA_GATE_RANK, GLA_QK), GLA_GATE_RANK ** -0.5),
        'gla_b_g2': nrm(ks[8], (L, GLA_QK), 0.1),
        'gla_norm': 1.0 + nrm(ks[9], (L, GLA_DV), 0.05),
        'ml_i_bias': nrm(ks[10], (L, MLSTM_HEADS), 0.1),
        'ml_f_bias': jnp.linspace(3.0, 6.0, MLSTM_HEADS, dtype=f32) + nrm(ks[11], (L, MLSTM_HEADS), 0.1),
        'ml_norm': 1.0 + nrm(ks[12], (L, MLSTM_DV), 0.05),
        'gdn_conv': nrm(ks[13], (L, GDN_CONV, GDN_QKV), GDN_CONV ** -0.5),
        'gdn_a_log': jnp.log(jax.random.uniform(ks[14], (L, GDN_HEADS), f32, 1.0, 16.0)),
        'gdn_dt_bias': dt + jnp.log(-jnp.expm1(-dt)),
        'gdn_norm': 1.0 + nrm(ks[16], (L, GDN_DV), 0.05),
        'w_out': nrm(ks[17], (L, D_MODEL, D_MODEL), D_MODEL ** -0.5),
        'w_ffn_up': nrm(ks[18], (L, D_MODEL, 2 * D_FF), D_MODEL ** -0.5),
        'w_ffn_down': nrm(ks[19], (L, D_FF, D_MODEL), D_FF ** -0.5),
        'norm_final': 1.0 + nrm(ks[20], (D_MODEL,), 0.05),
    }

def reference(x, c, ada_w, ada_b, norm_mix, norm_ffn, w_in, gla_w_g2, gla_b_g2, gla_norm,
              ml_i_bias, ml_f_bias, ml_norm, gdn_conv, gdn_a_log, gdn_dt_bias, gdn_norm,
              w_out, w_ffn_up, w_ffn_down, norm_final):
    c_act = jax.nn.silu(c)
    for l in range(DEPTH):
        mod = (c_act @ ada_w[l] + ada_b[l])[:, None, :]
        sh_mix, sc_mix, gt_mix, sh_ffn, sc_ffn, gt_ffn = jnp.split(mod, 6, axis=-1)
        h = rmsnorm(x, norm_mix[l]) * (1.0 + sc_mix) + sh_mix
        x = x + gt_mix * hybrid_mixer(h, w_in[l], gla_w_g2[l], gla_b_g2[l], gla_norm[l],
                                      ml_i_bias[l], ml_f_bias[l], ml_norm[l],
                                      gdn_conv[l], gdn_a_log[l], gdn_dt_bias[l], gdn_norm[l], w_out[l])
        h = rmsnorm(x, norm_ffn[l]) * (1.0 + sc_ffn) + sh_ffn
        x = x + gt_ffn * swiglu(h, w_ffn_up[l], w_ffn_down[l])
    return rmsnorm(x, norm_final)


_drawn_inputs = setup_inputs


def setup_inputs(seed=0):
    import zlib

    import numpy as np

    out = dict(_drawn_inputs(seed))
    spreads = {}
    factors = {'norm_mix': 3.428,
     'norm_ffn': 3.828,
     'gla_w_g2': 3.17,
     'gla_b_g2': 8.0,
     'gla_norm': 8.0,
     'ml_i_bias': 64.0,
     'ml_norm': 47.427,
     'gdn_norm': 8.0}
    for name, (base, spread) in spreads.items():
        noise = np.random.default_rng([zlib.crc32(name.encode()), seed]).standard_normal(out[name].shape)
        drawn = base * np.exp(spread * noise) if base else spread * noise
        out[name] = jnp.asarray(drawn.astype(out[name].dtype))
    for name, factor in factors.items():
        out[name] = (out[name] * factor).astype(out[name].dtype)
    return out
```

```python
from contextlib import ExitStack

import concourse.bass as bass
from concourse import mybir

F32 = mybir.dt.float32
F32R = mybir.dt.float32r
ALU = mybir.AluOpType
ACT = mybir.ActivationFunctionType
ds = bass.ds

P = 128
D = 1024
S = 1024
EPS = 1e-6
KT = D // P
NT = S // P
GLA_H, GLA_DK, GLA_DV, GLA_RANK, GLA_GATE_NORM, SUB = 4, 128, 256, 16, 16.0, 16
ML_H, ML_DK, ML_DV, ML_CAP, ML_M_INIT = 4, 128, 256, 15.0, -1e30
GDN_H, GDN_DK, GDN_DV, GDN_TAPS = 8, 128, 128, 4
D_FF = 2816
NEG = -1e30
LN_DK = -2.4260151319598084

_SIZES = [512, 512, D, D, GLA_RANK, 512, 512, D, D, ML_H, ML_H, 3 * D, D, GDN_H, GDN_H, 3 * D]
_NAMES = ["gla_q", "gla_k", "gla_v", "gla_r", "gla_glr", "ml_q", "ml_k", "ml_v", "ml_o", "ml_i", "ml_f",
          "gdn_qkv", "gdn_z", "gdn_a", "gdn_b", "merge"]
COL = {n: sum(_SIZES[:i]) for i, n in enumerate(_NAMES)}
D_IN = sum(_SIZES)
SMALL = GLA_RANK + 2 * ML_H + 2 * GDN_H
LEVELS = [2, 4, 8, 16, 32, 64]
HALF = S // 2


class Count:

    def __init__(self, sem, step=1):
        self.sem, self.step, self.n = sem, step, 0

    def inc(self, ins):
        self.n += self.step
        ins.then_inc(self.sem, self.step)

    def wait(self, eng):
        if self.n:
            eng.wait_ge(self.sem, self.n)


def hybrid_block(nc, x, c, ada_w, ada_b, norm_mix, norm_ffn, w_in, gla_w_g2, gla_b_g2, gla_norm,
                 ml_i_bias, ml_f_bias, ml_norm, gdn_conv, gdn_a_log, gdn_dt_bias, gdn_norm,
                 w_out, w_ffn_up, w_ffn_down, norm_final, out):
    ctx = ExitStack()
    with ctx:
        _build(ctx, nc, x[0], c, ada_w[0], ada_b[0], norm_mix[0], norm_ffn[0], w_in[0], gla_w_g2[0], gla_b_g2[0],
               gla_norm[0], ml_i_bias[0], ml_f_bias[0], ml_norm[0], gdn_conv[0], gdn_a_log[0], gdn_dt_bias[0],
               gdn_norm[0], w_out[0], w_ffn_up[0], w_ffn_down[0], norm_final, out[0])


def _build(ctx, nc, x, c, ada_w, ada_b, norm_mix, norm_ffn, w_in, gla_w_g2, gla_b_g2, gla_norm,
           ml_i_bias, ml_f_bias, ml_norm, gdn_conv, gdn_a_log, gdn_dt_bias, gdn_norm,
           w_out, w_ffn_up, w_ffn_down, norm_final, out):

    def sb(name, shape, dt=F32, stack=ctx):
        return stack.enter_context(nc.sbuf_tensor(name, shape, dt))

    sems = {}

    def sem(name):
        if name not in sems:
            sems[name] = ctx.enter_context(nc.semaphore(name))
        return sems[name]

    def end_section():
        nc.all_engine_barrier()
        nums = sorted(s.num for s in sems.values())
        start = prev = nums[0]
        for n in nums[1:] + [None]:
            if n != prev + 1 if n is not None else True:
                nc.sync.sem_clear(range(start, prev + 1))
                start = n
            prev = n
        nc.all_engine_barrier()

    banks = [ctx.enter_context(nc.psum_tensor(f"bank{i}", [P, 512], F32)) for i in range(8)]

    ident = sb("ident", [P, P])
    tri = sb("tri", [P, P])
    ones = sb("ones", [P, P])
    eps = sb("eps", [P, 1])
    ln_dk = sb("ln_dk", [P, 1])
    last_row = sb("last_row", [P, P])
    neg_mask = sb("neg_mask", [P, 2, P])
    level_mask = sb("level_mask", [P, len(LEVELS), 64])
    pair_mask = sb("pair_mask", [P, P])

    gates_dram = nc.dram_tensor("gates_scratch", (2, D), F32, kind="Internal").ap()
    y_dram = nc.dram_tensor("y_scratch", (3, S, D), F32, kind="Internal").ap()

    h_hi = sb("h_hi", [P, KT, S], F32R)
    h_lo = sb("h_lo", [P, KT, S], F32R)
    mod_col = sb("mod_col", [P, 4, KT])
    conv_col = sb("conv_col", [P, GDN_TAPS * 24])
    w_raw = sb("w_raw", [P, 2, KT, P])
    inproj = ExitStack()
    w_buf = {n: [sb(f"w{n}_{h}", [P, KT, w], F32R, stack=inproj if n == "C" else ctx) for h in ("hi", "lo")]
             for n, w in (("A", 256), ("B", 256), ("C", P))}

    A_W, B_W, C_W = (w_buf[n] for n in "ABC")

    with nc.Block() as block:
        @block.gpsimd
        def _(pool):
            made = Count(sem("const_made"))

            def fill(ap, v):
                made.inc(pool.memset(ap, v))

            fill(ident[:], 0.0)
            fill(tri[:], 1.0)
            fill(ones[:], 1.0)
            fill(eps[:], EPS)
            fill(ln_dk[:], LN_DK)
            fill(last_row[:], 1.0)
            fill(neg_mask[:], 0.0)
            fill(level_mask[:], 1.0)
            fill(pair_mask[:], 0.0)
            made.wait(pool)

            def select(ap, pattern, base, mult, op, value):
                made.inc(pool.affine_select(out=ap, in_=ap, pattern=pattern, base=base, channel_multiplier=mult,
                                            compare_op=op, fill=value))

            select(ident[:], [[-1, P]], 0, 1, ALU.not_equal, 1.0)
            select(tri[:], [[1, P]], 0, -1, ALU.is_ge, 0.0)
            select(last_row[:], [[0, P]], -(P - 1), 1, ALU.is_ge, 0.0)
            select(neg_mask[:, 0], [[1, P]], -1, -1, ALU.is_ge, NEG)
            select(neg_mask[:, 1], [[1, P]], 0, -1, ALU.is_ge, NEG)
            select(pair_mask[:].rearrange("p (n r) -> p n r", r=2)[:, :, 1], [[-2, P // 2]], 0, 1,
                   ALU.not_equal, -1.0)
            for v, b in enumerate(LEVELS):
                m = level_mask[:, v].rearrange("p (n b) -> p n b", b=b)
                select(m, [[-2 * b, 64 // b], [0, b]], -b, 1, ALU.is_ge, 0.0)
                made.wait(pool)
                select(m, [[2 * b, 64 // b], [0, b]], 2 * b - 1, -1, ALU.is_ge, 0.0)
            made.wait(pool)
    end_section()

    mod = ExitStack()
    ROWS = 48 + 3 * KT
    vec_rows = sb("vec_rows", [ROWS, P], stack=mod)
    vec_col = sb("vec_col", [P, ROWS], stack=mod)
    conv_rows = sb("conv_rows", [GDN_TAPS * 24, P], stack=mod)
    c_col = vec_col[:, 64:72]
    c_sig = sb("c_sig", [P, KT], stack=mod)
    c_act = sb("c_act", [P, KT], stack=mod)
    c_wide = sb("c_wide", [P, KT, P], stack=mod)
    ada_b_col = vec_col[:, 0:48].rearrange("p (a k) -> p a k", k=KT)
    ada_b_bc = sb("ada_b_bc", [P, 2, D], stack=mod)
    gain_col = vec_col[:, 48:64].rearrange("p (a k) -> p a k", k=KT)
    gate_bc = sb("gate_bc", [P, 2, D], stack=mod)
    ada_ring = sb("ada_ring", [P, 3, KT, 512], stack=mod)
    ADA = [(kind, part, half) for kind, part in (("col", 0), ("col", 1), ("bc", 2), ("col", 3), ("col", 4), ("bc", 5))
           for half in range(2)]
    ada_v = ada_w.rearrange("(k p) n -> p k n", p=P)
    with nc.Block() as block:
        @block.sync
        def _(sp):
            for lo, n, v in ((0, 48, ada_b), (48, 8, norm_mix), (56, 8, norm_ffn), (64, 8, c[0])):
                sp.dma_start(vec_rows[lo:lo + n, :], v.rearrange("(k p) -> k p", p=P)).then_inc(sem("vec_in"), 16)
            sp.dma_start(conv_rows[:], gdn_conv.rearrange("j (k p) -> (j k) p", p=P)).then_inc(sem("vec_in"), 16)
            for i in range(2):
                sp.dma_start(ada_b_bc[:, i], ada_b[(3 * i + 2) * D:(3 * i + 3) * D].partition_broadcast(P)) \
                    .then_inc(sem("bc_in"), 16)
            for n, (kind, part, half) in enumerate(ADA):
                if n >= 3:
                    sp.wait_ge(sem("ada_used"), n - 2)
                o = part * D + half * 512
                sp.dma_start(ada_ring[:, n % 3], ada_v[:, :, o:o + 512]).then_inc(sem(f"ada_in{n % 3}"), 16)
            sp.wait_ge(sem("mod_done"), 10)
            sp.dma_start(gates_dram.unsqueeze(0), gate_bc[0:1]).then_inc(sem("gates_out"), 16)
            sp.wait_ge(sem("gates_out"), 16)

        @block.scalar
        def _(act):
            act.wait_ge(sem("cols_up"), 2)
            nc.scalar.activation(vec_col[:], banks[7][:, 0:ROWS], ACT.Copy).then_inc(sem("cols"), 1)
            nc.scalar.activation(conv_col[:], banks[6][:, 0:GDN_TAPS * 24], ACT.Copy).then_inc(sem("cols"), 1)
            act.wait_ge(sem("cols"), 2)
            nc.scalar.activation(c_sig[:], c_col, ACT.Exp, scale=-1.0).then_inc(sem("c_exp"), 1)
            act.wait_ge(sem("c_act"), 3)
            for k in range(KT):
                nc.scalar.activation(c_wide[:, k], ones[:], ACT.Copy, scale=c_act[:, k:k + 1]).then_inc(sem("c_wide"), 1)

        @block.vector
        def _(dve):
            done = Count(sem("c_act"))
            dve.wait_ge(sem("c_exp"), 1)
            done.inc(dve.tensor_scalar(c_sig[:], c_sig[:], 1.0, None, ALU.add))
            done.wait(dve)
            done.inc(dve.reciprocal(c_sig[:], c_sig[:]))
            done.wait(dve)
            done.inc(dve.tensor_tensor(c_act[:], c_col, c_sig[:], ALU.mult))
            dve.wait_ge(sem("bc_in"), 32)
            own = Count(sem("mod_done"))
            dve.wait_ge(sem("ada_used"), 4)
            for i, part in ((0, 1), (2, 4)):
                if i == 2:
                    dve.wait_ge(sem("ada_used"), 10)
                own.inc(dve.scalar_tensor_tensor(mod_col[:, i], banks[0][:, part * KT:part * KT + KT], 1.0,
                                                 ada_b_col[:, part], ALU.add, ALU.add))
                own.wait(dve)
                own.inc(dve.tensor_tensor(mod_col[:, i], mod_col[:, i], gain_col[:, i // 2], ALU.mult))
                own.inc(dve.tensor_tensor(mod_col[:, i + 1], banks[0][:, (part - 1) * KT:part * KT],
                                          ada_b_col[:, part - 1], ALU.add))
            for i in range(2):
                for half in range(2):
                    dve.wait_ge(sem("ada_used"), 6 * i + half + 5)
                    own.inc(dve.tensor_tensor(gate_bc[:, i, half * 512:half * 512 + 512], banks[1 + 2 * i + half][:],
                                              ada_b_bc[:, i, half * 512:half * 512 + 512], ALU.add))

        @block.tensor
        def _(pe):
            pe.wait_ge(sem("vec_in"), 80)
            nc.tensor.transpose(banks[7][:, 0:ROWS], vec_rows[:], ident[0:ROWS, 0:ROWS]).then_inc(sem("cols_up"), 1)
            nc.tensor.transpose(banks[6][:, 0:GDN_TAPS * 24], conv_rows[:], ident[0:96, 0:96]) \
                .then_inc(sem("cols_up"), 1)
            pe.wait_ge(sem("c_act"), 3)
            for n, (kind, part, half) in enumerate(ADA):
                pe.wait_ge(sem(f"ada_in{n % 3}"), 16 * (n // 3 + 1))
                if part == 3 and half == 0:
                    pe.wait_ge(sem("mod_done"), 3)
                if kind == "col":
                    for j in range(4):
                        o = part * KT + half * 4 + j
                        for k in range(KT):
                            mm = nc.tensor.matmul(banks[0][:, o:o + 1], ada_ring[:, n % 3, k, j * P:j * P + P],
                                                  c_act[:, k:k + 1], start=(k == 0), stop=(k == KT - 1))
                    mm.then_inc(sem("ada_used"), 1)
                else:
                    if n == 4:
                        pe.wait_ge(sem("c_wide"), KT)
                    b = banks[1 + 2 * (part // 3) + half]
                    for k in range(KT):
                        mm = nc.tensor.matmul(b[:], c_wide[:, k], ada_ring[:, n % 3, k], start=(k == 0),
                                              stop=(k == KT - 1))
                    mm.then_inc(sem("ada_used"), 1)
    end_section()
    mod.close()

    done_tf = []

    def to_feature_major(src, t_scale, mod_i, load=None):
        norm = mod_i is not None
        st = ExitStack()
        done_tf.append(mod_i)
        full = sb(f"tf_full{len(done_tf)}", [P, 2, 512], stack=st)
        junk = sb(f"tf_junk{len(done_tf)}", [P, D], stack=st)
        ss = sb(f"tf_ss{len(done_tf)}", [P, NT], stack=st)
        rstd = sb(f"tf_rstd{len(done_tf)}", [P, NT], stack=st)
        with nc.Block() as block:
            @block.sync
            def _(sp):
                if load is not None:
                    for t in range(NT):
                        sp.dma_start(src[:, t], load[t * P:t * P + P, :]).then_inc(sem(f"rows_in{t}"), 16)

            @block.scalar
            def _(act):
                if norm:
                    nc.scalar.preload_act_table_set("natural_log_exp_and_others")
                    rms = Count(sem("tf_ln"))
                    for t in range(NT):
                        if load is not None:
                            act.wait_ge(sem(f"rows_in{t}"), 16)
                        if t:
                            act.wait_ge(sem("tf_square"), t)
                        nc.scalar.activation(junk[:], src[:, t], ACT.Square, accum_out=ss[:, t:t + 1]) \
                            .then_inc(sem("tf_square"), 1)
                        act.wait_ge(sem("tf_square"), t + 1)
                        rms.inc(nc.scalar.activation(ss[:, t:t + 1], ss[:, t:t + 1], ACT.Ln, scale=1.0 / D, bias=eps[:]))
                        rms.wait(act)
                        nc.scalar.activation(rstd[:, t:t + 1], ss[:, t:t + 1], ACT.Exp, scale=-0.5) \
                            .then_inc(sem("tf_rstd"), 1)
                for n in range(2 * KT):
                    act.wait_ge(sem("tf_full"), n + 1)
                    k, half = n % KT, n // KT
                    nc.scalar.activation(h_hi[:, k, half * 512:half * 512 + 512], full[:, n % 2], ACT.Copy) \
                        .then_inc(sem("tf_hi"), 1)

            @block.vector
            def _(dve):
                if norm:
                    for t in range(NT):
                        dve.wait_ge(sem("tf_rstd"), t + 1)
                        dve.tensor_scalar(t_scale[:, t], src[:, t], rstd[:, t:t + 1], None, ALU.mult) \
                            .then_inc(sem("tf_rows"), 1)
                for n in range(2 * KT):
                    k, half = n % KT, n // KT
                    dve.wait_ge(sem("tf_up"), n + 1)
                    if n >= 2:
                        dve.wait_ge(sem("tf_lo"), n - 1)
                    b = banks[n % 4][:]
                    if norm:
                        dve.tensor_scalar(full[:, n % 2], b, mod_col[:, mod_i, k:k + 1],
                                          mod_col[:, mod_i + 1, k:k + 1], ALU.mult, ALU.add) \
                            .then_inc(sem("tf_full"), 1)
                    else:
                        dve.tensor_copy(full[:, n % 2], b).then_inc(sem("tf_full"), 1)
                    dve.wait_ge(sem("tf_hi"), n + 1)
                    dve.tensor_tensor(h_lo[:, k, half * 512:half * 512 + 512], full[:, n % 2],
                                      h_hi[:, k, half * 512:half * 512 + 512].bitcast(F32), ALU.subtract) \
                        .then_inc(sem("tf_lo"), 1)

            @block.tensor
            def _(pe):
                for n in range(2 * KT):
                    k, half = n % KT, n // KT
                    if norm:
                        pe.wait_ge(sem("tf_rows"), 4 * half + 4)
                    if n >= 4:
                        pe.wait_ge(sem("tf_full"), n - 3)
                    for j in range(4):
                        tp = nc.tensor.transpose(banks[n % 4][:, j * P:j * P + P],
                                                 t_scale[:, 4 * half + j, k * P:k * P + P], ident[:])
                    tp.then_inc(sem("tf_up"), 1)
        end_section()
        st.close()

    pro = ExitStack()
    x_rows = sb("x_rows", [P, NT, D], stack=pro)
    to_feature_major(x_rows, x_rows, 0, load=x)
    pro.close()

    w_v = w_in.rearrange("(k p) n -> p k n", p=P)

    def load_half(sp, i, src):
        sp.dma_start(w_raw[:, i, :, 0:src.shape[2]], src).then_inc(sem(f"w_in{i}"), 16)

    def qk_cols(q0, k0):
        return [w_v[:, :, ds(q0, P)], w_v[:, :, ds(k0, P)]]

    def split(pool, i, buf, width, own, gate=None, gated=None):
        hi, lo = (w[:, :, i * width:(i + 1) * width] for w in buf)
        raw = w_raw[:, i, :, 0:width]
        if gate is not None:
            gated.inc(pool.tensor_tensor(raw, raw, gate.unsqueeze(1).broadcast_to([P, KT, width]), ALU.mult))
            gated.wait(pool)
        own.inc(pool.tensor_copy(hi, raw))
        own.wait(pool)
        own.inc(pool.tensor_tensor(lo, raw, hi.bitcast(F32), ALU.subtract))
        own.wait(pool)

    PASSES = [(0, 0), (0, 1), (1, 0)]

    def token_major(bank, t, buf, n0, n1, steps, n_out=0):
        for s in steps:
            k, (wp, hp) = s // 3, PASSES[s % 3]
            mm = nc.tensor.matmul(bank[:, n_out:n_out + n1 - n0], (h_hi, h_lo)[hp][:, k, t * P:t * P + P],
                                  buf[wp][:, k, n0:n1], start=(s == 0), stop=(s == 3 * KT - 1))
        return mm

    def feature_major(bank, half, buf, n0, steps):
        for s in steps:
            k, (wp, hp) = s // 3, PASSES[s % 3]
            mm = nc.tensor.matmul(bank[:], buf[wp][:, k, n0:n0 + P],
                                  (h_hi, h_lo)[hp][:, k, half * HALF:half * HALF + HALF],
                                  start=(s == 0), stop=(s == 3 * KT - 1))
        return mm

    gdn_g = sb("gdn_g", [P, 4, NT, GDN_H], stack=inproj)
    ml_g = sb("ml_g", [P, 6, NT, ML_H], stack=inproj)
    glr_t = sb("glr_t", [GLA_RANK, S], stack=inproj)
    gt = ExitStack()
    pg = sb("pg", [P, NT, SMALL], stack=gt)
    gb = sb("gb", [P, 2 * ML_H + 2 * GDN_H], stack=gt)
    u1 = sb("u1", [P, NT, 16], stack=gt)
    u2 = sb("u2", [P, NT, 16], stack=gt)
    u3 = sb("u3", [P, NT, 16], stack=gt)
    rate = sb("rate", [P, GDN_H], stack=gt)
    capped = sb("capped", [P, NT, 2 * ML_H], stack=gt)
    mt1 = sb("mt1", [P, NT, 2 * ML_H], stack=gt)
    logs = sb("logs", [P, NT * (GDN_H + ML_H)], stack=gt)
    cums = sb("cums", [P, NT * (GDN_H + ML_H)], stack=gt)
    tots = sb("tots", [P, NT * (GDN_H + ML_H)], stack=gt)
    rows = sb("rows", [ML_H, 3, S], stack=gt)
    m_col = sb("m_col", [P, NT, ML_H], stack=gt)
    m_end = sb("m_end", [P, NT, ML_H], stack=gt)
    mx = sb("mx", [P, 3, NT, ML_H], stack=gt)
    NG, NM = NT * GDN_H, NT * ML_H
    logs_g = logs[:, 0:NG].rearrange("p (t h) -> p t h", h=GDN_H)
    logs_m = logs[:, NG:].rearrange("p (t h) -> p t h", h=ML_H)
    cum_g = cums[:, 0:NG].rearrange("p (t h) -> p t h", h=GDN_H)
    cum_m = cums[:, NG:].rearrange("p (t h) -> p t h", h=ML_H)
    tot_g = tots[:, 0:NG].rearrange("p (t h) -> p t h", h=GDN_H)
    tot_m = tots[:, NG:].rearrange("p (t h) -> p t h", h=ML_H)

    def over_tiles(row):
        n = row.shape[1]
        return row.unsqueeze(1).broadcast_to([P, NT, n])

    with nc.Block() as block:
        @block.sync
        def _(sp):
            for o, v in ((0, ml_i_bias), (4, ml_f_bias), (8, gdn_dt_bias), (16, gdn_a_log)):
                sp.dma_start(gb[:, o:o + v.shape[0]], v.partition_broadcast(P)).then_inc(sem("bias_in"), 16)
            for o, name, n in ((0, "gla_glr", 16), (16, "ml_i", 8), (24, "gdn_a", 16)):
                sp.dma_start(w_raw[:, 0, :, o:o + n], w_v[:, :, COL[name]:COL[name] + n]).then_inc(sem("w_small"), 16)
            first = qk_cols(COL["gdn_qkv"], COL["gdn_qkv"] + D)
            load_half(sp, 1, first[1])
            sp.wait_ge(sem("w_split"), 2)
            load_half(sp, 0, first[0])

        @block.gpsimd
        def _(pool):
            own = Count(sem("w_split"))
            pool.wait_ge(sem("w_small"), 48)
            split(pool, 0, C_W, SMALL, own)
            for i in (1, 0):
                pool.wait_ge(sem(f"w_in{i}"), 16)
                split(pool, i, A_W, P, own)

        @block.tensor
        def _(pe):
            pe.wait_ge(sem("w_split"), 2)
            for t in range(NT):
                mm = token_major(banks[0], t, C_W, 0, SMALL, range(3 * KT), n_out=t * SMALL)
            mm.then_inc(sem("pg_up"), 1)
            pe.wait_ge(sem("pg"), 1)
            for t in range(NT):
                tp = nc.tensor.transpose(banks[1 + t // 4][0:GLA_RANK, t % 4 * P:t % 4 * P + P], pg[:, t, 0:16],
                                         ident[:])
            tp.then_inc(sem("glr_up"), 1)
            pe.wait_ge(sem("logs"), 1)
            nc.tensor.matmul(banks[3][:, 0:NG + NM], tri[:], logs[:], start=True, stop=True).then_inc(sem("cum_up"), 1)
            nc.tensor.matmul(banks[4][:, 0:NG + NM], ones[:], logs[:], start=True, stop=True).then_inc(sem("cum_up"), 1)
            pe.wait_ge(sem("glr"), 2)
            for q in range(2):
                for t in range(NT):
                    src = logs_m[:, t] if q == 0 else capped[:, t, 0:ML_H]
                    bank = banks[(1, 5)[q] + t // 4]
                    tp = nc.tensor.transpose(bank[0:ML_H, t % 4 * P:t % 4 * P + P], src, ident[:])
            tp.then_inc(sem("rows_up"), 1)
            pe.wait_ge(sem("m_row"), 1)
            for t in range(NT):
                tp = nc.tensor.transpose(banks[0][:, t * ML_H:(t + 1) * ML_H], rows[:, 2, t * P:t * P + P],
                                         ident[0:ML_H, 0:ML_H])
            tp.then_inc(sem("m_up"), 1)
            pe.wait_ge(sem("m_col"), 1)
            nc.tensor.matmul(banks[7][:, 0:NM], last_row[:], m_col[:].rearrange("p t h -> p (t h)"), start=True,
                             stop=True).then_inc(sem("m_end_up"), 1)

        @block.scalar
        def _(act):
            A = nc.scalar.activation
            own = Count(sem("gate_act"))
            nc.scalar.preload_act_table_set("natural_log_exp_and_others")
            act.wait_ge(sem("bias_in"), 64)
            own.inc(A(rate[:], gb[:, 16:24], ACT.Exp))
            act.wait_ge(sem("glr_up"), 1)
            for h in range(2):
                A(glr_t[:, h * HALF:(h + 1) * HALF], banks[1 + h][0:GLA_RANK, :], ACT.Copy).then_inc(sem("glr"), 1)
            act.wait_ge(sem("pre_cap"), 1)
            own.inc(A(capped[:], capped[:], ACT.Tanh, scale=1.0 / ML_CAP))
            act.wait_ge(sem("pre_exp"), 2)
            own.inc(A(u2[:], u2[:], ACT.Abs))
            own.wait(act)
            own.inc(A(u2[:], u2[:], ACT.Exp, scale=-1.0))
            own.inc(A(mt1[:, :, ML_H:], capped[:, :, ML_H:], ACT.Exp, scale=-1.0))
            own.wait(act)
            own.inc(A(u2[:], u2[:], ACT.Ln, bias=1.0))
            own.inc(A(mt1[:, :, ML_H:], mt1[:, :, ML_H:], ACT.Ln, bias=1.0))
            act.wait_ge(sem("ln_beta"), 1)
            own.inc(A(gdn_g[:, 2], gdn_g[:, 1], ACT.Exp))
            act.wait_ge(sem("rows_up"), 1)
            for q in range(2):
                for h in range(2):
                    own.inc(A(rows[:, q, h * HALF:(h + 1) * HALF], banks[(1, 5)[q] + h][0:ML_H, :], ACT.Copy))
            act.wait_ge(sem("ml_exps"), 1)
            own.inc(A(ml_g[:, 3:6], mx[:], ACT.Exp))

        @block.vector
        def _(dve):
            own = Count(sem("gate_dve"))
            dve.wait_ge(sem("pg_up"), 1)
            dve.tensor_copy(pg[:].rearrange("p t n -> p (t n)"), banks[0][:, 0:NT * SMALL]).then_inc(sem("pg"), 1)
            dve.wait_ge(sem("pg"), 1)
            dve.wait_ge(sem("bias_in"), 64)
            dve.tensor_tensor(capped[:], pg[:, :, 16:24], over_tiles(gb[:, 0:8]), ALU.add).then_inc(sem("pre_cap"), 1)
            own.inc(dve.tensor_tensor(u1[:, :, 0:8], pg[:, :, 24:32], over_tiles(gb[:, 8:16]), ALU.add))
            own.inc(dve.tensor_scalar(u1[:, :, 8:16], pg[:, :, 32:40], -1.0, None, ALU.mult))
            own.wait(dve)
            dve.tensor_copy(u2[:], u1[:]).then_inc(sem("pre_exp"), 1)
            own.inc(dve.tensor_scalar(u3[:], u1[:], 0.0, None, ALU.max))
            dve.wait_ge(sem("gate_act"), 2)
            dve.tensor_scalar(capped[:], capped[:], ML_CAP, None, ALU.mult).then_inc(sem("pre_exp"), 1)
            dve.wait_ge(sem("gate_act"), 7)
            own.inc(dve.tensor_tensor(u3[:], u3[:], u2[:], ALU.add))
            own.wait(dve)
            dve.tensor_scalar(gdn_g[:, 1], u3[:, :, 8:16], -1.0, None, ALU.mult).then_inc(sem("ln_beta"), 1)
            own.inc(dve.scalar_tensor_tensor(logs_g, u3[:, :, 0:8], -1.0, over_tiles(rate[:]), ALU.mult, ALU.mult))
            dve.tensor_scalar(logs_m, mt1[:, :, ML_H:], -1.0, None, ALU.mult).then_inc(sem("logs_m"), 1)
            dve.wait_ge(sem("logs_m"), 1)
            own.wait(dve)
            dve.tensor_copy(m_end[:], logs_m).then_inc(sem("logs"), 1)
            dve.wait_ge(sem("cum_up"), 2)
            own.inc(dve.tensor_copy(cums[:], banks[3][:, 0:NG + NM]))
            own.inc(dve.tensor_copy(tots[:], banks[4][:, 0:NG + NM]))
            own.wait(dve)
            own.inc(dve.tensor_copy(gdn_g[:, 0], cum_g))
            own.inc(dve.tensor_copy(gdn_g[:, 3], tot_g))
            dve.wait_ge(sem("gate_act"), 12)
            dve.tensor_tensor_scan(rows[:, 2], rows[:, 0], rows[:, 1], ML_M_INIT, ALU.add, ALU.max) \
                .then_inc(sem("m_row"), 1)
            dve.wait_ge(sem("m_up"), 1)
            dve.tensor_copy(m_col[:], banks[0][:, 0:NM].rearrange("p (t h) -> p t h", h=ML_H)).then_inc(sem("m_col"), 1)
            dve.wait_ge(sem("m_col"), 1)
            dve.wait_ge(sem("m_end_up"), 1)
            own.inc(dve.tensor_copy(m_end[:], banks[7][:, 0:NM].rearrange("p (t h) -> p t h", h=ML_H)))
            own.inc(dve.memset(ml_g[:, 2, 0], ML_M_INIT))
            own.inc(dve.scalar_tensor_tensor(ml_g[:, 0], m_col[:], -1.0, cum_m, ALU.mult, ALU.add))
            own.inc(dve.tensor_tensor(ml_g[:, 1], capped[:, :, 0:ML_H], cum_m, ALU.subtract))
            own.wait(dve)
            own.inc(dve.tensor_copy(ml_g[:, 2, 1:NT], m_end[:, 0:NT - 1]))
            own.inc(dve.tensor_tensor(mx[:, 0], tot_m, m_end[:], ALU.subtract))
            own.inc(dve.tensor_scalar(mx[:, 2], m_col[:], -1.0, None, ALU.mult))
            own.wait(dve)
            own.inc(dve.tensor_scalar(ml_g[:, 0], ml_g[:, 0], LN_DK, None, ALU.add))
            own.inc(dve.tensor_tensor(mx[:, 1], mx[:, 0], ml_g[:, 2], ALU.add))
            own.wait(dve)
            dve.tensor_tensor(mx[:, 0], mx[:, 0], ml_g[:, 1], ALU.add).then_inc(sem("ml_exps"), 1)
    end_section()
    gt.close()

    mixers = ExitStack()

    def mb(name, shape, dt=F32):
        return sb(name, shape, dt, stack=mixers)

    kq = mb("kq", [P, 2, S])
    v_t = mb("v_t", [P, S])
    gdn_m = mb("gdn_m", [P, NT, GDN_DV])
    conv_in = mb("conv_in", [P, 2, S + GDN_TAPS - 1])
    pair_buf = mb("pair_buf", [P, 20 * P])
    conv_acc = pair_buf[:, 12 * P:20 * P]
    gh = mb("gh", [P, 4, NT])
    conv_w = mb("conv_w", [P, GDN_TAPS, 3])
    lnss = mb("lnss", [P, 2, NT])
    gq = mb("gq", [P, 4, NT])
    gex = mb("gex", [P, 3, NT])
    qg = mb("qg", [P, S])
    kg = mb("kg", [P, S])
    vg = mb("vg", [P, NT, GLA_DV + 1])
    mg = mb("mg", [P, NT, GLA_DV])
    sig = mb("sig", [P, 2, 256])
    gain_g = mb("gain_g", [P, 2, GLA_DV])
    gain_d = mb("gain_d", [P, GDN_DV])
    wts = pair_buf[:, 0 * P:4 * P].rearrange("p (c n) -> p c n", c=2)
    at = pair_buf[:, 4 * P:8 * P].rearrange("p (c n) -> p c n", c=2)
    qdec = pair_buf[:, 12 * P:14 * P].rearrange("p (c n) -> p c n", c=2)
    xm = pair_buf[:, 8 * P:10 * P].rearrange("p (c n) -> p c n", c=2)
    xmt = pair_buf[:, 10 * P:12 * P].rearrange("p (c n) -> p c n", c=2)
    pm = mb("pm", [P, len(LEVELS), 2, P])
    kend = pair_buf[:, 14 * P:16 * P].rearrange("p (c n) -> p c n", c=2)
    vbeta = pair_buf[:, 16 * P:18 * P].rearrange("p (c n) -> p c n", c=2)
    rhs = pair_buf[:, 18 * P:19 * P]
    vnew = pair_buf[:, 19 * P:20 * P]
    state_d = mb("state_d", [P, P])
    junk = mb("junk", [P, 256])
    ybuf = mb("ybuf", [P, 2, 256])
    rs = mb("rs", [P, 4])
    w_g2 = mb("w_g2", [GLA_RANK, P])
    b_g2 = mb("b_g2", [P, 1])
    la = pair_buf[:, 0 * P:8 * P]
    gabs = pair_buf[:, 8 * P:12 * P]
    cum = mb("cum", [P, P])
    edge = mb("edge", [P, 2, NT])
    last16 = mb("last16", [P, 1])
    dl_col = mb("dl_col", [P, NT])
    dq = mb("dq", [P, P])
    ke = mb("ke", [P, P])
    kt_sub = mb("kt_sub", [P, NT, P])
    qd = mb("qd", [P, 2, P])
    sc = mb("sc", [P, P])
    kend_g = mb("kend_g", [P, P])
    state_g = mb("state_g", [P, GLA_DV + 1])
    mh = mb("mh", [P, 6, NT])

    G = banks[0:2]
    M = banks[2:8]

    class Steps:

        def __init__(self, eng, own):
            self.eng, self.own, self.counts = eng, own, {}

        def __call__(self, ins, name=None):
            n = self.counts.setdefault(name or self.own, Count(sem(name or self.own)))
            n.inc(ins)
            n.wait(self.eng)

        def free_bank(self, ins, u):
            ins.then_inc(sem(f"proj_read{u % 2}"), 1)
            self.eng.wait_ge(sem(f"proj_read{u % 2}"), u // 2 + 1)

    def gla_cols(br, f):
        q, k, v, r = (COL[n] for n in (("gla_q", "gla_k", "gla_v", "gla_r") if br == "gla" else
                                       ("ml_q", "ml_k", "ml_v", "ml_o")))
        g = COL["merge"] + (0 if br == "gla" else D)
        return [qk_cols(f * P + q, f * P + k)] + \
            [qk_cols(f * 256 + v, f * 256 + (v + P))] + \
            [qk_cols(f * 256 + (r + o), f * 256 + (g + o)) for o in (0, P)]

    def gdn_cols(h):
        o = COL["gdn_qkv"]
        return [qk_cols(h * P + o, h * P + (o + D)),
                [w_v[:, :, ds(h * P + (o + 2 * D + i), 64)] for i in (0, 64)],
                qk_cols(h * P + COL["gdn_z"], h * P + (COL["merge"] + 2 * D))]

    BEATS1, CHUNK2, PRE2 = 22, 5, 6
    U1 = 28
    U2 = 14

    def mixer_section(br, f, h, next_h, prefetch):
        groups = []
        units = []

        def add_units(g, kind, span):
            units.extend((g, kind, i) for i in span)

        if br:
            groups += [(n, s, 256) for n, s in zip("ABAB", gla_cols(br, f))]
            for g, (kind, n) in enumerate((("qk", 4), ("v", NT), ("rg", NT), ("rg", NT))):
                add_units(g, kind, range(n))
        u0, g0 = len(units), len(groups)
        if next_h is not None:
            qk, v, zg = gdn_cols(next_h)
            groups += [("A", qk, 256), ("B", zg, 256), ("C", v, P)]
            add_units(g0, "gqk", range(4))
            add_units(g0 + 1, "zg", range(4))
            add_units(g0 + 2, "gv", range(2))
            add_units(g0 + 1, "zg", range(4, NT))
        n_units = len(units)
        if prefetch is not None:
            groups.append(("A", prefetch, 256))
        first_unit = {g: min(u for u in range(n_units) if units[u][0] == g) for g, _, _ in units}
        last_unit = {g: max(u for u in range(n_units) if units[u][0] == g) for g, _, _ in units}

        def gate_units(u):
            return sum(units[j][1] in ("rg", "zg") for j in range(u))

        def piece(pe, n):
            u, part = divmod(n, 3)
            g, kind, i = units[u]
            if part == 0:
                if first_unit[g] == u and g:
                    pe.wait_ge(sem("w_split"), 4 * g)
                if u >= 2:
                    pe.wait_ge(sem(f"proj_read{u % 2}"), u // 2)
            steps = range(8 * part, 8 * part + 8)
            buf = w_buf[groups[g][0]]
            if kind in ("qk", "gqk", "gv"):
                mm = feature_major(G[u % 2], i % 2, buf, (i // 2) * P, steps)
            else:
                mm = token_major(G[u % 2], i, buf, 0, 256, steps)
            if part == 2:
                mm.then_inc(sem(f"proj{u % 2}"), 1)

        def proj_ready(eng, u):
            eng.wait_ge(sem(f"proj{u % 2}"), u // 2 + 1)

        def act_unit(act, step, u):
            if not 0 <= u < n_units:
                return
            _, kind, i = units[u]
            b = G[u % 2]
            A = nc.scalar.activation
            proj_ready(act, u)
            half = (i % 2) * HALF
            if kind == "qk":
                step.free_bank(A((qg, kg)[i // 2][:, half:half + HALF], b[:], ACT.Copy), u)
            elif kind == "gqk":
                o = GDN_TAPS - 1 + half
                step.free_bank(A(conv_in[:, i // 2 % 2, o:o + HALF], b[:], ACT.Copy), u)
            elif kind == "gv":
                o = GDN_TAPS - 1 + half
                act.wait_ge(sem("conv_ss"), 1)
                step.free_bank(A(conv_in[:, 0, o:o + HALF], b[:], ACT.Copy), u)
            elif kind == "v":
                step.free_bank(A(vg[:, i, 0:GLA_DV], b[:, 0:256], ACT.Copy), u)
            else:
                n = gate_units(u)
                if n >= 2:
                    act.wait_ge(sem("sig_used"), n - 1)
                step(A(sig[:, n % 2], b[:, 0:256], ACT.Exp, scale=-1.0), "sig_exp")

        def dve_unit(dve, step, u, stage):
            if not 0 <= u < n_units:
                return
            g, kind, i = units[u]
            if kind not in ("rg", "zg"):
                return
            n = gate_units(u)
            ex, eg = sig[:, n % 2, 0:P], sig[:, n % 2, P:2 * P]
            j = g % 2 if br else 0
            if kind == "zg":
                factor, gain = gdn_m[:, i], gain_d[:]
            else:
                factor = mg[:, i, j * P:j * P + P]
                gain = gain_g[:, 0 if br == "gla" else 1, j * P:j * P + P]
            if stage == 0:
                dve.wait_ge(sem("sig_exp"), n + 1)
                if kind == "rg" and br == "ml":
                    step.free_bank(dve.tensor_copy(factor, gain), u)
                else:
                    step.free_bank(dve.tensor_tensor(factor, G[u % 2][:, 0:P], gain, ALU.mult), u)
                step(dve.tensor_scalar(eg, eg, 1.0, None, ALU.add))
                step(dve.scalar_tensor_tensor(ex, ex, 1.0, eg, ALU.add, ALU.mult))
            elif stage == 1:
                step(dve.reciprocal(ex, ex))
            else:
                step(dve.tensor_tensor(factor, factor, ex, ALU.mult), "sig_used")

        def pair(ap, b, r):
            return ap.rearrange("p c (n r b) -> p c n r b", r=2, b=b)[:, :, :, r, :]

        def one(ap, b, r):
            return ap.rearrange("p (n r b) -> p n r b", r=2, b=b)[:, :, r, :]

        def gdn_pe(pe, d, j):
            mm = nc.tensor.matmul
            if j == 0:
                if d:
                    pe.wait_ge(sem("gdn_at"), d)
                for c in range(2):
                    t = (2 * d + c) * P
                    last = mm(M[0][:, c * 256:c * 256 + 256], kq[:, 0, t:t + P], kq[:, :, t:t + P], start=True,
                              stop=True)
                last.then_inc(sem("gdn_kq"), 1)
                if d:
                    pe.wait_ge(sem("gdn_eq"), d)
                for c in range(2):
                    for q in range(2):
                        last = mm(M[1][:, (2 * c + q) * P:(2 * c + q + 1) * P],
                                  gq[:, q, 2 * d + c:2 * d + c + 1].broadcast_to([P, P]), ident[:], start=True,
                                  stop=True)
                last.then_inc(sem("gdn_row"), 1)
                if d:
                    pe.wait_ge(sem("gdn_kv"), d)
                for i, src in enumerate((kq[:, 0], v_t[:])):
                    for c in range(2):
                        t = (2 * d + c) * P
                        last = nc.tensor.transpose(M[2][:, (2 * i + c) * P:(2 * i + c + 1) * P], src[:, t:t + P],
                                                   ident[:])
                last.then_inc(sem("gdn_tr"), 1)
            elif j == 3:
                pe.wait_ge(sem("gdn_xt"), 7 * d + 1)
                for c in range(2):
                    last = nc.tensor.transpose(M[3][:, c * P:c * P + P], xmt[:, c], ident[:])
                last.then_inc(sem("gdn_x1"), 1)
            elif 4 <= j < 16:
                v = (j - 4) // 2
                b = LEVELS[v]
                if j % 2 == 0:
                    pe.wait_ge(sem("gdn_x"), 6 * d + v + 1)
                    pe.wait_ge(sem("gdn_xt"), 7 * d + v + 1)
                    for c in range(2):
                        last = mm(M[3][:, c * 64:c * 64 + 64], at[:, c, 0:P], one(xm[:, c], b, 0), start=True, stop=True)
                    last.then_inc(sem("gdn_p"), 1)
                else:
                    pe.wait_ge(sem("gdn_pm"), 6 * d + v + 1)
                    for c in range(2):
                        if v < len(LEVELS) - 1:
                            mm(M[3][:, 128 + c * 64:192 + c * 64], xmt[:, c], one(pm[:, v, c], b, 0), start=True,
                               stop=True)
                        last = mm(M[3][:, 256 + c * 64:320 + c * 64], pm[:, v, c], one(xmt[:, c], b, 1), start=True,
                                  stop=True)
                    last.then_inc(sem("gdn_q"), 1)
            elif j >= 16:
                c, s = divmod(j - 16, 3)
                t = 2 * d + c
                if s == 0:
                    pe.wait_ge(sem("gdn_s"), t + 1)
                    mm(M[4][:, 0:P], kq[:, 0, t * P:t * P + P], state_d[:], start=True, stop=True) \
                        .then_inc(sem("gdn_ks"), 1)
                elif s == 1:
                    pe.wait_ge(sem("gdn_r"), t + 1)
                    pe.wait_ge(sem("gdn_xt"), 7 * d + 7)
                    mm(M[4][:, P:2 * P], xmt[:, c], rhs[:], start=True, stop=True).then_inc(sem("gdn_vn"), 1)
                else:
                    if t:
                        pe.wait_ge(sem("gdn_y"), t)
                    pe.wait_ge(sem("gdn_qd"), d + 1)
                    mm(M[5][:, 0:P], qdec[:, c], state_d[:], start=True, stop=False)
                    pe.wait_ge(sem("gdn_vv"), t + 1)
                    mm(M[5][:, 0:P], at[:, c, P:2 * P], vnew[:], start=False, stop=True)
                    mm(M[4][:, 2 * P:3 * P], kend[:, c], vnew[:], start=True, stop=True).then_inc(sem("gdn_os"), 1)

        def gdn_act(act, step, d, j):
            A = nc.scalar.activation
            if j == 0:
                act.wait_ge(sem("gdn_tr"), d + 1)
                for c in range(2):
                    t = 2 * d + c
                    step(A(kend[:, c], M[2][:, c * P:c * P + P], ACT.Copy, scale=gex[:, 1, t:t + 1]))
                    step(A(vbeta[:, c], M[2][:, (2 + c) * P:(3 + c) * P], ACT.Copy, scale=gh[:, 2, t:t + 1]),
                         "gdn_kv" if c else None)
            elif j == 1:
                act.wait_ge(sem("gdn_w"), d + 1)
                for c in range(2):
                    t = 2 * d + c
                    step(A(wts[:, c], wts[:, c], ACT.Exp, bias=gq[:, 2, t:t + 1]), "gdn_e" if c else None)
                step(A(qdec[:], M[1][:].rearrange("p (c q t) -> p c q t", c=2, q=2)[:, :, 1], ACT.Exp), "gdn_eq")
            elif j >= 16:
                c, s = divmod(j - 16, 3)
                t = 2 * d + c
                if s == 1:
                    act.wait_ge(sem("gdn_vn"), t + 1)
                    step(A(vnew[:], M[4][:, P:2 * P], ACT.Copy), "gdn_vv")
                elif s == 2:
                    act.wait_ge(sem("gdn_os"), t + 1)
                    if t:
                        act.wait_ge(sem("gdn_y"), t)
                    step(A(junk[:, 0:P], M[5][:, 0:P], ACT.Square, accum_out=rs[:, 0:1]))
                    step(A(rs[:, 1:2], rs[:, 0:1], ACT.Ln, scale=1.0 / GDN_DV, bias=eps[:]))
                    step(A(rs[:, 2:3], rs[:, 1:2], ACT.Exp, scale=-0.5), "gdn_rms")

        def gdn_dve(dve, step, d, j):
            tt, stt = dve.tensor_tensor, dve.scalar_tensor_tensor
            if j == 0:
                if d == 0:
                    step(dve.memset(state_d[:], 0.0), "gdn_s")
                dve.wait_ge(sem("gdn_row"), d + 1)
                step(tt(wts[:].rearrange("p c (q t) -> p c q t", q=2),
                        M[1][:].rearrange("p (c q t) -> p c q t", c=2, q=2),
                        neg_mask[:].unsqueeze(1).broadcast_to([P, 2, 2, P]), ALU.add), "gdn_w")
            elif j == 1:
                dve.wait_ge(sem("gdn_e"), d + 1)
                dve.wait_ge(sem("gdn_kq"), d + 1)
                step(tt(at[:].rearrange("p c n -> p (c n)"), M[0][:], wts[:].rearrange("p c n -> p (c n)"), ALU.mult),
                     "gdn_at")
                step(tt(xmt[:], at[:, :, 0:P], pair_mask[:].unsqueeze(1).broadcast_to([P, 2, P]), ALU.mult))
                step(tt(xmt[:], xmt[:], ident[:].unsqueeze(1).broadcast_to([P, 2, P]), ALU.add), "gdn_xt")
                dve.wait_ge(sem("gdn_eq"), d + 1)
                step(tt(qdec[:], qdec[:], kq[:, 1, 2 * d * P:2 * (d + 1) * P].rearrange("p (c t) -> p c t", c=2),
                        ALU.mult), "gdn_qd")
            elif j == 3:
                dve.wait_ge(sem("gdn_x1"), d + 1)
                step(dve.tensor_copy(xm[:].rearrange("p c n -> p (c n)"), M[3][:, 0:2 * P]), "gdn_x")
            elif 4 <= j < 16:
                v = (j - 4) // 2
                b = LEVELS[v]
                n = 64 // b

                def cols(o):
                    return M[3][:, o:o + 128].rearrange("p (c n b) -> p c n b", c=2, b=b)

                if j % 2 == 0:
                    dve.wait_ge(sem("gdn_p"), 6 * d + v + 1)
                    mask = level_mask[:, v].rearrange("p (n b) -> p n b", b=b).unsqueeze(1).broadcast_to([P, 2, n, b])
                    step(tt(pair(pm[:, v], b, 0), cols(0), mask, ALU.mult), "gdn_pm")
                else:
                    dve.wait_ge(sem("gdn_q"), 6 * d + v + 1)
                    if v < len(LEVELS) - 1:
                        step(tt(pair(xm[:], b, 0), pair(xm[:], b, 0), cols(128), ALU.subtract), "gdn_x")
                    step(tt(pair(xmt[:], b, 1), pair(xmt[:], b, 1), cols(256), ALU.subtract), "gdn_xt")
            elif j >= 16:
                c, s = divmod(j - 16, 3)
                t = 2 * d + c
                if s == 0:
                    dve.wait_ge(sem("gdn_ks"), t + 1)
                    dve.wait_ge(sem("gdn_kv"), d + 1)
                    step(stt(rhs[:], M[4][:, 0:P], gq[:, 3, t:t + 1], vbeta[:, c], ALU.mult, ALU.add), "gdn_r")
                elif s == 2:
                    dve.wait_ge(sem("gdn_os"), t + 1)
                    step(stt(state_d[:], state_d[:], gex[:, 2, t:t + 1], M[4][:, 2 * P:3 * P], ALU.mult, ALU.add),
                         "gdn_s")
                    dve.wait_ge(sem("gdn_rms"), t + 1)
                    if t >= 2:
                        dve.wait_ge(sem(f"y_out{t % 2}"), 16 * (t // 2))
                    step(stt(ybuf[:, t % 2, 0:P], M[5][:, 0:P], rs[:, 2:3], gdn_m[:, t], ALU.mult, ALU.mult), "gdn_y")

        def head_pe(pe):
            if br == "gla":
                pe.wait_ge(sem("g2_in"), 32)
                for half in range(2):
                    nc.tensor.matmul(M[half][:], w_g2[:], glr_t[:, half * HALF:half * HALF + HALF], start=True,
                                     stop=True).then_inc(sem("gla_g"), 1)

        def head_act(act, step):
            if br == "gla":
                for half in range(2):
                    s = slice(half * HALF, half * HALF + HALF)
                    act.wait_ge(sem("gla_g"), half + 1)
                    step(nc.scalar.activation(gabs[:], M[half][:], ACT.Abs, bias=b_g2[:]), "gla_abs")
                    step(nc.scalar.activation(gabs[:], gabs[:], ACT.Exp, scale=-1.0))
                    act.wait_ge(sem("gla_min"), half + 1)
                    step(nc.scalar.activation(gabs[:], gabs[:], ACT.Ln, bias=1.0), "gla_ln")
                    act.wait_ge(sem("gla_la"), half + 1)

        def head_dve(dve, step):
            step(dve.memset(state_g[:], 0.0), "g_s")
            if br == "gla":
                step(dve.memset(edge[:], 0.0))
                for half in range(2):
                    s = slice(half * HALF, half * HALF + HALF)
                    dve.wait_ge(sem("gla_abs"), half + 1)
                    step(dve.tensor_scalar(la[:, s], M[half][:], b_g2[:], 0.0, ALU.add, ALU.min), "gla_min")
                    dve.wait_ge(sem("gla_ln"), half + 1)
                    step(dve.tensor_tensor(la[:, s], la[:, s], gabs[:], ALU.subtract), "gla_la")
            else:
                mv = ml_g[:].rearrange("p q t h -> p (q t) h")
                step(dve.tensor_copy(mh[:].rearrange("p q t -> p (q t)").unsqueeze(2), mv[:, :, ds(f, 1)]), "ml_mh")

        def prep_act(act, step, c, stage):
            A = nc.scalar.activation
            if stage == 0:
                act.wait_ge(sem("gla_cum"), c + 1)
                if c:
                    act.wait_ge(sem("g_sc"), c)
                if c >= 2:
                    act.wait_ge(sem("g_os"), c - 1)
                step(A(dq[:], dq[:], ACT.Exp, scale=1.0 / GLA_GATE_NORM, bias=ln_dk[:]))
                step(A(qd[:, c % 2], cum[:], ACT.Exp, scale=1.0 / GLA_GATE_NORM, bias=ln_dk[:]))
                step(A(dl_col[:, c:c + 1], last16[:], ACT.Exp), "gla_dl")
                step(A(ke[:], cum[:], ACT.Exp, scale=-1.0 / GLA_GATE_NORM, bias=last16[:]), "gla_ee")
            for i in range(4 * stage, 4 * stage + 4):
                n = SUB * (i + 1)
                step(A(kt_sub[:, i, 0:n], cum[:, 0:n], ACT.Exp, scale=-1.0 / GLA_GATE_NORM,
                       bias=edge[:, 1, i:i + 1]), "gla_ek" if i == P // SUB - 1 else None)

        def prep_dve(dve, step, c):
            cs = slice(c * P, c * P + P)
            if c:
                dve.wait_ge(sem("gla_ek"), c)
            step(dve.tensor_tensor_scan(cum[:], ones[:], la[:, cs], 0.0, ALU.mult, ALU.add))
            step(dve.tensor_copy(edge[:, 0, 1:NT], cum[:, SUB - 1:P - 1:SUB]))
            step(dve.tensor_scalar(edge[:, 1], edge[:, 0], 1.0 / GLA_GATE_NORM, None, ALU.mult))
            step(dve.tensor_scalar(last16[:], cum[:, P - 1:P], 1.0 / GLA_GATE_NORM, None, ALU.mult))
            if c:
                dve.wait_ge(sem("g_sc"), c)
            step(dve.tensor_tensor(dq[:].rearrange("p (n s) -> p n s", s=SUB),
                                   cum[:].rearrange("p (n s) -> p n s", s=SUB),
                                   edge[:, 0].unsqueeze(2).broadcast_to([P, NT, SUB]), ALU.subtract), "gla_cum")

        def prep_pool(pool, step, c):
            cs = slice(c * P, c * P + P)
            if c == 0:
                pool.wait_ge(sem("proj_read1"), 2)
                pool.wait_ge(sem("proj_read0"), 2)
            pool.wait_ge(sem("gla_ee"), c + 1)
            step(pool.tensor_tensor(dq[:], qg[:, cs], dq[:], ALU.mult))
            step(pool.tensor_tensor(qd[:, c % 2], qg[:, cs], qd[:, c % 2], ALU.mult))
            step(pool.tensor_tensor(ke[:], kg[:, cs], ke[:], ALU.mult))
            pool.wait_ge(sem("gla_ek"), c + 1)
            step(pool.tensor_tensor(kt_sub[:], kt_sub[:], kg[:, cs].unsqueeze(1).broadcast_to([P, NT, P]), ALU.mult),
                 "gla_prep")

        def chunk_pe(pe, c, stage):
            mm = nc.tensor.matmul
            cs = slice(c * P, c * P + P)
            n = GLA_DV if br == "gla" else GLA_DV + 1
            if stage == 0:
                if c:
                    pe.wait_ge(sem("g_scd"), c)
                    pe.wait_ge(sem("g_kend"), c)
                if br == "gla":
                    pe.wait_ge(sem("gla_prep"), c + 1)
                    if c == 0:
                        pe.wait_ge(sem("gla_la"), 2)
                    for i in range(P // SUB):
                        mm(M[0][:, i * SUB:i * SUB + SUB], kt_sub[:, i], dq[:, i * SUB:i * SUB + SUB], start=True,
                           stop=True)
                    nc.tensor.transpose(M[2][:, 0:P], ke[:], ident[:]).then_inc(sem("g_sc"), 1)
                else:
                    if c == 0:
                        pe.wait_ge(sem("ml_mh"), 1)
                    if c:
                        pe.wait_ge(sem("ml_eq"), c)
                    mm(M[0][:, 0:P], kg[:, cs], qg[:, cs], start=True, stop=True)
                    mm(M[1][:, 0:P], mh[:, 0, c:c + 1].broadcast_to([P, P]), ident[:], start=True, stop=True)
                    nc.tensor.transpose(M[2][:, 0:P], kg[:, cs], ident[:]).then_inc(sem("g_sc"), 1)
            else:
                pe.wait_ge(sem("g_scd"), c + 1)
                pe.wait_ge(sem("g_s"), c + 1)
                if c:
                    pe.wait_ge(sem("g_y"), c)
                if br == "ml":
                    pe.wait_ge(sem("ml_qd"), c + 1)
                mm(M[3][:, 0:n], sc[:], vg[:, c, 0:n], start=True, stop=False)
                mm(M[3][:, 0:n], qd[:, c % 2], state_g[:, 0:n], start=False, stop=True)
                pe.wait_ge(sem("g_kend"), c + 1)
                mm(M[4][:, 0:n], kend_g[:], vg[:, c, 0:n], start=True, stop=True).then_inc(sem("g_os"), 1)

        def chunk_act(act, step, c, stage):
            A = nc.scalar.activation
            if stage == 0:
                act.wait_ge(sem("g_sc"), c + 1)
                if c:
                    act.wait_ge(sem("g_os"), c)
                if br == "gla":
                    step(A(kend_g[:], M[2][:, 0:P], ACT.Copy), "g_kend")
                else:
                    step(A(kend_g[:], M[2][:, 0:P], ACT.Copy, scale=mh[:, 3, c:c + 1]), "g_kend")
                    act.wait_ge(sem("ml_w"), c + 1)
                    step(A(dq[:], dq[:], ACT.Exp, bias=mh[:, 1, c:c + 1]), "ml_e")
                    step(A(qd[:, c % 2], M[1][:, 0:P], ACT.Exp, bias=mh[:, 2, c:c + 1]), "ml_eq")
            else:
                act.wait_ge(sem("g_os"), c + 1)
                if c:
                    act.wait_ge(sem("g_y"), c)
                step(A(junk[:], M[3][:, 0:GLA_DV], ACT.Square, accum_out=rs[:, 0:1]))
                if br == "gla":
                    step(A(rs[:, 1:2], rs[:, 0:1], ACT.Ln, scale=1.0 / GLA_DV, bias=eps[:]))
                    step(A(rs[:, 2:3], rs[:, 1:2], ACT.Exp, scale=-0.5), "g_rms")
                else:
                    step(A(rs[:, 1:2], M[3][:, GLA_DV:GLA_DV + 1], ACT.Abs), "ml_den")
                    act.wait_ge(sem("ml_ms"), c + 1)
                    step(A(rs[:, 2:3], rs[:, 2:3], ACT.Ln, scale=1.0 / GLA_DV, bias=eps[:]))
                    step(A(rs[:, 2:3], rs[:, 2:3], ACT.Exp, scale=-0.5), "g_rms")

        def chunk_dve(dve, step, c, stage):
            tt, stt = dve.tensor_tensor, dve.scalar_tensor_tensor
            n = GLA_DV if br == "gla" else GLA_DV + 1
            if stage == 0:
                dve.wait_ge(sem("g_sc"), c + 1)
                if br == "gla":
                    if c:
                        dve.wait_ge(sem("g_os"), c)
                    step(tt(sc[:], M[0][:, 0:P], tri[:], ALU.mult), "g_scd")
                else:
                    step(tt(dq[:], M[1][:, 0:P], neg_mask[:, 1], ALU.add), "ml_w")
                    dve.wait_ge(sem("ml_e"), c + 1)
                    step(tt(sc[:], M[0][:, 0:P], dq[:], ALU.mult), "g_scd")
                    dve.wait_ge(sem("ml_eq"), c + 1)
                    step(tt(qd[:, c % 2], qg[:, c * P:c * P + P], qd[:, c % 2], ALU.mult), "ml_qd")
            else:
                dve.wait_ge(sem("g_os"), c + 1)
                if br == "gla":
                    dve.wait_ge(sem("gla_dl"), c + 1)
                decay = dl_col[:, c:c + 1] if br == "gla" else mh[:, 4, c:c + 1]
                step(stt(state_g[:, 0:n], state_g[:, 0:n], decay, M[4][:, 0:n], ALU.mult, ALU.add), "g_s")
                if br == "ml":
                    dve.wait_ge(sem("ml_den"), c + 1)
                    step(tt(rs[:, 1:2], rs[:, 1:2], mh[:, 5, c:c + 1], ALU.max))
                    step(dve.reciprocal(rs[:, 3:4], rs[:, 1:2]))
                    step(tt(rs[:, 2:3], rs[:, 3:4], rs[:, 3:4], ALU.mult))
                    step(tt(rs[:, 2:3], rs[:, 2:3], rs[:, 0:1], ALU.mult), "ml_ms")
                dve.wait_ge(sem("g_rms"), c + 1)
                if br == "ml":
                    step(tt(rs[:, 2:3], rs[:, 2:3], rs[:, 3:4], ALU.mult))
                dve.wait_ge(sem(f"y_out{c % 2}"), 16 * ((NT + c) // 2))
                step(stt(ybuf[:, c % 2], M[3][:, 0:GLA_DV], rs[:, 2:3], mg[:, c], ALU.mult, ALU.mult), "g_y")

        CONV_AT = (7, 18, 31)

        def conv_dve(dve, step, b):
            for j in range(3):
                o = b - CONV_AT[j]
                e = conv_in[:, j % 2, GDN_TAPS - 1:]
                if o in range(GDN_TAPS):
                    src = conv_in[:, j % 2, o:o + S]
                    w = conv_w[:, o, j:j + 1]
                    if o == 0:
                        for u in (u0 + (0, 2, 8)[j], u0 + (1, 3, 9)[j]):
                            dve.wait_ge(sem(f"proj_read{u % 2}"), u // 2 + 1)
                        step(dve.tensor_scalar(conv_acc[:], src, w, None, ALU.mult))
                    else:
                        step(dve.scalar_tensor_tensor(conv_acc[:], src, w, conv_acc[:], ALU.mult, ALU.add),
                             "conv" if o == GDN_TAPS - 1 else None)
                elif o == 6:
                    dve.wait_ge(sem("conv_e"), j + 1)
                    step(dve.scalar_tensor_tensor(e, conv_acc[:], 0.0, e, ALU.min, ALU.subtract), "conv_ls")
                elif o == 9:
                    dve.wait_ge(sem("conv_sig"), j + 1)
                    step(dve.tensor_tensor((kq[:, 1], kq[:, 0], v_t[:])[j], conv_acc[:], e, ALU.mult), "conv_silu")

        def conv_act(act, step, b):
            A = nc.scalar.activation
            for j in range(3):
                o = b - CONV_AT[j]
                e = conv_in[:, j % 2, GDN_TAPS - 1:]
                if o == 3:
                    act.wait_ge(sem("conv"), j + 1)
                    step(A(e, conv_acc[:], ACT.Abs))
                elif o == 4:
                    step(A(e, e, ACT.Exp, scale=-1.0))
                elif o == 5:
                    step(A(e, e, ACT.Ln, bias=1.0), "conv_e")
                elif o == 7:
                    act.wait_ge(sem("conv_ls"), j + 1)
                    step(A(e, e, ACT.Exp), "conv_sig")
                elif o == 10 and j < 2:
                    act.wait_ge(sem("conv_silu"), j + 1)
                    step(A(e, (kq[:, 1], kq[:, 0])[j], ACT.Square), "conv_sq")

        def conv_pe(pe, b):
            for j in range(2):
                if b == CONV_AT[j] + 12:
                    pe.wait_ge(sem("conv_sq"), j + 1)
                    for t in range(NT):
                        o = GDN_TAPS - 1 + t * P
                        mm = nc.tensor.matmul(M[5][:, j * NT + t:j * NT + t + 1], conv_in[:, j % 2, o:o + P], ones[:, 0:1],
                                              start=True, stop=True)
                    mm.then_inc(sem("conv_ss"), 1)

        def gates_act(act, step, b):
            if b == 32:
                act.wait_ge(sem("conv_ss"), 2)
                step(nc.scalar.activation(lnss[:].rearrange("p q t -> p (q t)"), M[5][:, 0:2 * NT], ACT.Ln,
                                          bias=eps[:]), "gate_ln")
            if b == 34:
                act.wait_ge(sem("gate_pre"), 1)
                step(nc.scalar.activation(gex[:], gex[:], ACT.Exp), "gate_e")

        def gates_dve(dve, step, b):
            tt, stt = dve.tensor_tensor, dve.scalar_tensor_tensor
            if b == 6:
                wv = conv_col[:].rearrange("p (j i h) -> p (j i) h", i=3, h=GDN_H)
                step(dve.tensor_copy(conv_w[:].rearrange("p j i -> p (j i)").unsqueeze(2), wv[:, :, ds(next_h, 1)]))
            if b == 33:
                gv = gdn_g[:].rearrange("p q t h -> p (q t) h")
                step(dve.tensor_copy(gh[:].rearrange("p q t -> p (q t)").unsqueeze(2), gv[:, :, ds(next_h, 1)]))
                dve.wait_ge(sem("gate_ln"), 1)
                step(stt(gq[:, 2], lnss[:, 1], -0.5, gh[:, 0], ALU.mult, ALU.subtract))
                step(stt(gq[:, 1], lnss[:, 0], -0.5, gh[:, 0], ALU.mult, ALU.add))
                step(dve.tensor_scalar(gq[:, 1], gq[:, 1], LN_DK, None, ALU.add))
                step(stt(gex[:, 0], lnss[:, 1], -0.5, gh[:, 0], ALU.mult, ALU.add))
                step(tt(gq[:, 0], gex[:, 0], gh[:, 1], ALU.add))
                step(tt(gex[:, 1], gh[:, 3], gq[:, 2], ALU.add))
                step(dve.tensor_copy(gex[:, 2], gh[:, 3]), "gate_pre")
            if b == 35:
                dve.wait_ge(sem("gate_e"), 1)
                step(stt(gq[:, 3], gex[:, 0], -1.0, gh[:, 2], ALU.mult, ALU.mult))

        n1 = 4 * BEATS1 if br else 0
        n2 = PRE2 + CHUNK2 * NT + 1
        pieces1 = 3 * U1 if br else 0
        pieces2 = 3 * (n_units - (U1 if br else 0))
        if br:
            LOAD_AT = {1: 0, 2: 8, 3: 20, 4: 44, 5: 68, 6: n1 + 1, 7: n1 + 10}
            SPLIT_AT = {1: (0, 0), 2: (13, 13), 3: (37, 37), 4: (61, 61), 5: (n1 - 3, n1 - 3),
                        6: (n1 + 9, n1 + 9), 7: (n1 + 14, n1 + 19)}
        else:
            LOAD_AT = {1: 0, 2: 1, 3: 2}
            SPLIT_AT = {1: (0, 0), 2: (1, 1), 3: (13, 13)}

        with nc.Block() as block:
            @block.sync
            def _(sp):
                if br == "gla":
                    sp.dma_start(w_g2[:], gla_w_g2[:, ds(f * P, P)]).then_inc(sem("g2_in"), 16)
                    sp.dma_start(b_g2[:], gla_b_g2.rearrange("(n a) -> n a", a=1)[ds(f * P, P), :]) \
                        .then_inc(sem("g2_in"), 16)
                for b in range(n1 + n2 + 1):
                    for g in range(1, len(groups)):
                        if LOAD_AT[g] == b:
                            for i in range(2):
                                if g >= 2:
                                    sp.wait_ge(sem("w_split"), 4 * (g - 2) + 2 * (i + 1))
                                load_half(sp, i, groups[g][1][i])
                    if not br:
                        continue
                    for t in range(NT):
                        if b == BEATS1 * (t // 2) + 19 + 3 * (t % 2):
                            sp.wait_ge(sem("gdn_y"), t + 1)
                            sp.dma_start(y_dram[2, t * P:t * P + P, ds(h * P, P)], ybuf[:, t % 2, 0:P]) \
                                .then_inc(sem(f"y_out{t % 2}"), 16)
                        if b == n1 + PRE2 + CHUNK2 * t + 4:
                            sp.wait_ge(sem("g_y"), t + 1)
                            sp.dma_start(y_dram[0 if br == "gla" else 1, t * P:t * P + P, ds(f * GLA_DV, GLA_DV)],
                                         ybuf[:, t % 2]).then_inc(sem(f"y_out{t % 2}"), 16)
                if br:
                    for i in range(2):
                        sp.wait_ge(sem(f"y_out{i}"), 16 * NT)

            @block.gpsimd
            def _(pool):
                own = Count(sem("w_split"))
                step = Steps(pool, "pool_step")
                for b in range(n1 + n2):
                    c, s = divmod(b - n1 - 3, CHUNK2)
                    if br == "gla" and s == 0 and 0 <= c < NT:
                        prep_pool(pool, step, c)
                    for g in range(1, len(groups)):
                        buf, _, width = groups[g]
                        for i in range(2):
                            if SPLIT_AT[g][i] != b:
                                continue
                            before = [k for k in range(g) if groups[k][0] == buf]
                            if before and i == 0:
                                u = last_unit[before[-1]]
                                pool.wait_ge(sem(f"proj{u % 2}"), u // 2 + 1)
                            pool.wait_ge(sem(f"w_in{i}"), 16 * g)
                            split(pool, i, w_buf[buf], width // 2, own)

            @block.tensor
            def _(pe):
                for b in range(n1):
                    gdn_pe(pe, b // BEATS1, b % BEATS1)
                    if b < pieces1:
                        piece(pe, b)
                for b in range(n2):
                    if br:
                        if b == 0:
                            head_pe(pe)
                        c, s = divmod(b - PRE2, CHUNK2)
                        if 0 <= c < NT and s in (0, 3):
                            chunk_pe(pe, c, s // 3)
                    if next_h is not None:
                        conv_pe(pe, b)
                    if b < pieces2:
                        piece(pe, pieces1 + b)

            @block.scalar
            def _(act):
                step = Steps(act, "act_step")
                nc.scalar.preload_act_table_set("natural_log_exp_and_others")
                for b in range(n1):
                    gdn_act(act, step, b // BEATS1, b % BEATS1)
                    if b % 3 == 0 and b // 3 <= U1:
                        act_unit(act, step, b // 3 - 1)
                for b in range(n2):
                    if br:
                        if b == 0:
                            head_act(act, step)
                        c, s = divmod(b - PRE2, CHUNK2)
                        if 0 <= c < NT and s in (0, 3):
                            chunk_act(act, step, c, s // 3)
                        c, s = divmod(b - 2, CHUNK2)
                        if br == "gla" and s < 2 and 0 <= c < NT:
                            prep_act(act, step, c, s)
                    if next_h is not None:
                        conv_act(act, step, b)
                        gates_act(act, step, b)
                    if b % 3 == 0 and b:
                        act_unit(act, step, u0 + b // 3 - 1)

            @block.vector
            def _(dve):
                step = Steps(dve, "dve_step")
                for b in range(n1):
                    gdn_dve(dve, step, b // BEATS1, b % BEATS1)
                    if 3 <= b < 3 * U1 + 3:
                        dve_unit(dve, step, b // 3 - 1, b % 3)
                for b in range(n2):
                    if br:
                        if b == 0:
                            head_dve(dve, step)
                        c, s = divmod(b - PRE2, CHUNK2)
                        if 0 <= c < NT and s in (0, 3):
                            chunk_dve(dve, step, c, s // 3)
                        c, s = divmod(b - 1, CHUNK2)
                        if br == "gla" and s == 0 and 0 <= c < NT:
                            prep_dve(dve, step, c)
                    if next_h is not None:
                        gates_dve(dve, step, b)
                        conv_dve(dve, step, b)
                    if b >= 3:
                        dve_unit(dve, step, u0 + b // 3 - 1, b % 3)
        end_section()

    with nc.Block() as block:
        @block.sync
        def _(sp):
            for i, v in enumerate((gla_norm, ml_norm)):
                sp.dma_start(gain_g[:, i], v.partition_broadcast(P)).then_inc(sem("gain_in"), 16)
            sp.dma_start(gain_d[:], gdn_norm.partition_broadcast(P)).then_inc(sem("gain_in"), 16)
            sp.wait_ge(sem("gain_in"), 48)

        @block.vector
        def _(dve):
            own = Count(sem("cleared"))
            own.inc(dve.memset(conv_in[:, :, 0:GDN_TAPS - 1], 0.0))
            own.inc(dve.memset(pm[:], 0.0))
            own.inc(dve.memset(kt_sub[:], 0.0))
            own.inc(dve.memset(vg[:], 1.0))
            own.wait(dve)
    end_section()
    mixer_section(None, None, None, 0, gla_cols("gla", 0)[0])
    with nc.Fori(0, GLA_H) as f:
        last = (f + 1) >> 2
        q, k = ((f + 1) * P + (last * (COL["ml_" + n] - COL["gla_" + n] - GLA_H * P) + COL["gla_" + n]) for n in "qk")
        mixer_section("gla", f, f, f + 1, qk_cols(q, k))
    with nc.Fori(0, ML_H - 1) as f:
        mixer_section("ml", f, f + GLA_H, f + (GLA_H + 1), gla_cols("ml", f + 1)[0])
    mixer_section("ml", ML_H - 1, GDN_H - 1, None, None)
    mixers.close()
    inproj.close()

    x1 = sb("x1", [P, NT, D])
    gates = sb("gates", [P, 2, D])
    between = ExitStack()
    rows_a = sb("rows_a", [P, NT, D], stack=between)
    y_parts = x1[:, 0:6].rearrange("p (a b) d -> p a b d", a=2)
    out_v = w_out.rearrange("(k p) n -> p k n", p=P)

    def out_cols(g):
        return [out_v[:, :, g * 256 + i:g * 256 + i + P] for i in (0, P)]

    with nc.Block() as block:
        @block.sync
        def _(sp):
            for t in range(NT):
                if t >= 2:
                    sp.wait_ge(sem("y_sum"), t - 1)
                sp.dma_start(y_parts[:, t % 2], y_dram[:, t * P:t * P + P, :].rearrange("b p d -> p b d")) \
                    .then_inc(sem(f"y_in{t % 2}"), 16)
            for i in range(2):
                load_half(sp, i, out_cols(0)[i])
                sp.dma_start(gates[:, i], gates_dram[i].partition_broadcast(P)).then_inc(sem("gates_in"), 16)
            sp.wait_ge(sem("gates_in"), 32)

        @block.gpsimd
        def _(pool):
            own, gated = Count(sem("w_split")), Count(sem("w_gated"))
            pool.wait_ge(sem("gates_in"), 32)
            for i in range(2):
                pool.wait_ge(sem(f"w_in{i}"), 16)
                split(pool, i, A_W, P, own, gates[:, 0, i * P:i * P + P], gated)

        @block.vector
        def _(dve):
            for t in range(NT):
                dve.wait_ge(sem(f"y_in{t % 2}"), 16 * (t // 2 + 1))
                dve.tensor_tensor(rows_a[:, t], y_parts[:, t % 2, 0], y_parts[:, t % 2, 1], ALU.add) \
                    .then_inc(sem("y_two"), 1)
                dve.wait_ge(sem("y_two"), t + 1)
                dve.tensor_tensor(rows_a[:, t], rows_a[:, t], y_parts[:, t % 2, 2], ALU.add).then_inc(sem("y_sum"), 1)
    end_section()
    to_feature_major(rows_a, rows_a, None)

    up_v = w_ffn_up.rearrange("(k p) n -> p k n", p=P)
    down_v = w_ffn_down.rearrange("(k p) n -> p k n", p=P)
    F_STEPS = D_FF // (2 * P)

    def up_cols(n):
        return [up_v[:, :, ds(n * P, P)], up_v[:, :, ds(n * P + D_FF, P)]]

    with nc.Block() as block:
        @block.sync
        def _(sp):
            sp.dma_start(x1[:], x.rearrange("(t p) d -> p t d", p=P)).then_inc(sem("x_in"), 16)
            groups = [out_cols(1), out_cols(2), out_cols(3), up_cols(0)]
            for g, cols in enumerate(groups):
                for i in range(2):
                    if g:
                        sp.wait_ge(sem("w_split"), 4 * (g - 1) + 2 * (i + 1))
                    load_half(sp, i, cols[i])

        @block.gpsimd
        def _(pool):
            own, gated = Count(sem("w_split")), Count(sem("w_gated"))
            for g in range(4):
                if g:
                    pool.wait_ge(sem("proj"), 8 * g)
                for i in range(2):
                    pool.wait_ge(sem(f"w_in{i}"), 16 * (g + 1))
                    c0 = (g + 1) * 256 + i * P
                    split(pool, i, (B_W, A_W)[g % 2], P, own, gates[:, 0, c0:c0 + P] if g < 3 else None, gated)

        @block.tensor
        def _(pe):
            for g in range(4):
                if g:
                    pe.wait_ge(sem("w_split"), 4 * g)
                for t in range(NT):
                    if g:
                        pe.wait_ge(sem("out_read"), NT * (g - 1) + t + 1)
                    token_major(banks[t], t, (A_W, B_W)[g % 2], 0, 256, range(3 * KT)).then_inc(sem("proj"), 1)

        @block.vector
        def _(dve):
            dve.wait_ge(sem("x_in"), 16)
            for g in range(4):
                cols = slice(g * 256, g * 256 + 256)
                for t in range(NT):
                    dve.wait_ge(sem("proj"), NT * g + t + 1)
                    dve.tensor_tensor(x1[:, t, cols], x1[:, t, cols], banks[t][:, 0:256], ALU.add) \
                        .then_inc(sem("out_read"), 1)
            dve.wait_ge(sem("out_read"), NT * 4)
    end_section()

    to_feature_major(x1, rows_a, 2)
    between.close()
    D_W = [sb(f"wD_{h}", [P, 2, D], F32R) for h in ("hi", "lo")]
    hid = [sb(f"hid_{h}", [P, 2, S], F32R) for h in ("hi", "lo")]
    e_buf = sb("e_buf", [P, 2, HALF])
    fin_gain = sb("fin_gain", [P, D])

    with nc.Block() as block:
        @block.sync
        def _(sp):
            sp.dma_start(fin_gain[:], norm_final.partition_broadcast(P)).then_inc(sem("gain_in"), 16)
            sp.wait_ge(sem("gain_in"), 16)
    end_section()

    def ffn_pass(i, last):
        UP, DOWN = banks[0:4], banks[4:8]
        n_groups = 2 if last else 3

        with nc.Block() as block:
            @block.sync
            def _(sp):
                for j, src in enumerate(up_cols(2 * i + 1)):
                    load_half(sp, j, src)
                for j in range(2):
                    sp.wait_ge(sem("w_split"), 2 * j + 2)
                    sp.dma_start(w_raw[:, j].rearrange("p k n -> p (k n)"), down_v[:, ds(2 * i + j, 1)].squeeze(1)
                                 if not isinstance(i, int) else down_v[:, 2 * i + j]).then_inc(sem(f"w_in{j}"), 16)
                if not last:
                    for j, src in enumerate(up_cols(2 * i + 2)):
                        sp.wait_ge(sem("w_split"), 4 + 2 * j + 2)
                        load_half(sp, j, src)

            @block.gpsimd
            def _(pool):
                own, gated = Count(sem("w_split")), Count(sem("w_gated"))
                for g in range(n_groups):
                    if g == 2:
                        pool.wait_ge(sem("up"), 4)
                    for j in range(2):
                        pool.wait_ge(sem(f"w_in{j}"), 16 * (g + 1))
                        if g == 1:
                            raw = w_raw[:, j].rearrange("p k n -> p (k n)")
                            gated.inc(pool.tensor_tensor(raw, raw, gates[:, 1], ALU.mult))
                            gated.wait(pool)
                            own.inc(pool.tensor_copy(D_W[0][:, j], raw))
                            own.wait(pool)
                            own.inc(pool.tensor_tensor(D_W[1][:, j], raw, D_W[0][:, j].bitcast(F32), ALU.subtract))
                            own.wait(pool)
                        else:
                            split(pool, j, (B_W, None, A_W)[g], P, own)

            @block.tensor
            def _(pe):
                for u in range(8):
                    k, half, gv = u // 4, u // 2 % 2, u % 2
                    if u == 4:
                        pe.wait_ge(sem("w_split"), 4)
                    if u >= 4:
                        pe.wait_ge(sem("hid_full"), u // 2 - 1)
                    feature_major(UP[u % 4], half, (A_W, B_W)[k], gv * P, range(3 * KT)).then_inc(sem("up"), 1)
                pe.wait_ge(sem("w_split"), 8)
                for n in range(2 * NT):
                    t, half = n // 2, n % 2
                    if n % NT == 0:
                        pe.wait_ge(sem("hid_lo"), 3 + n // NT)
                    if n >= 4:
                        pe.wait_ge(sem("down_read"), n - 3)
                    for s in range(6):
                        k, (wp, hp) = s // 3, PASSES[s % 3]
                        mm = nc.tensor.matmul(DOWN[n % 4][:], hid[hp][:, k, t * P:t * P + P],
                                              D_W[wp][:, k, half * HALF:half * HALF + HALF], start=(s == 0),
                                              stop=(s == 5))
                    mm.then_inc(sem("down"), 1)

            @block.scalar
            def _(act):
                nc.scalar.preload_act_table_set("natural_log_exp_and_others")
                for n in range(4):
                    k, half = n // 2, n % 2
                    act.wait_ge(sem("up"), 2 * n + 1)
                    if n >= 2:
                        act.wait_ge(sem("hid_lo"), n - 1)
                    nc.scalar.activation(e_buf[:, n % 2], UP[2 * n % 4][:], ACT.Exp, scale=-1.0) \
                        .then_inc(sem("gate_exp"), 1)
                    act.wait_ge(sem("hid_full"), n + 1)
                    nc.scalar.activation(hid[0][:, k, half * HALF:half * HALF + HALF], e_buf[:, n % 2], ACT.Copy) \
                        .then_inc(sem("hid_hi"), 1)

            @block.vector
            def _(dve):
                own = Count(sem("silu"))
                for n in range(4):
                    k, half = n // 2, n % 2
                    cols = slice(half * HALF, half * HALF + HALF)
                    e = e_buf[:, n % 2]
                    dve.wait_ge(sem("gate_exp"), n + 1)
                    own.inc(dve.tensor_scalar(e, e, 1.0, None, ALU.add))
                    own.wait(dve)
                    own.inc(dve.reciprocal(e, e))
                    own.wait(dve)
                    own.inc(dve.tensor_tensor(e, e, UP[2 * n % 4][:], ALU.mult))
                    own.wait(dve)
                    dve.wait_ge(sem("up"), 2 * n + 2)
                    dve.tensor_tensor(e, e, UP[2 * n % 4 + 1][:], ALU.mult).then_inc(sem("hid_full"), 1)
                    dve.wait_ge(sem("hid_full"), n + 1)
                    dve.wait_ge(sem("hid_hi"), n + 1)
                    dve.tensor_tensor(hid[1][:, k, cols], e, hid[0][:, k, cols].bitcast(F32), ALU.subtract) \
                        .then_inc(sem("hid_lo"), 1)
                for n in range(2 * NT):
                    t, half = n // 2, n % 2
                    acc = x1[:, t, half * HALF:half * HALF + HALF]
                    dve.wait_ge(sem("down"), n + 1)
                    dve.tensor_tensor(acc, acc, DOWN[n % 4][:], ALU.add).then_inc(sem("down_read"), 1)
                dve.wait_ge(sem("down_read"), 2 * NT)
        end_section()

    with nc.Fori(0, F_STEPS - 1) as i:
        ffn_pass(i, False)
    ffn_pass(F_STEPS - 1, True)

    f_ss = sb("f_ss", [P, NT])
    f_junk = sb("f_junk", [P, D])
    f_rstd = sb("f_rstd", [P, NT])
    with nc.Block() as block:
        @block.sync
        def _(sp):
            for t in range(NT):
                sp.wait_ge(sem("out_ready"), t + 1)
                sp.dma_start(out[t * P:t * P + P, :], x1[:, t]).then_inc(sem("out_stored"), 16)
            sp.wait_ge(sem("out_stored"), 16 * NT)

        @block.scalar
        def _(act):
            own = Count(sem("f_act"))
            nc.scalar.preload_act_table_set("natural_log_exp_and_others")
            for t in range(NT):
                own.inc(nc.scalar.activation(f_junk[:], x1[:, t], ACT.Square, accum_out=f_ss[:, t:t + 1]))
                own.wait(act)
                own.inc(nc.scalar.activation(f_ss[:, t:t + 1], f_ss[:, t:t + 1], ACT.Ln, scale=1.0 / D, bias=eps[:]))
                own.wait(act)
                nc.scalar.activation(f_rstd[:, t:t + 1], f_ss[:, t:t + 1], ACT.Exp, scale=-0.5) \
                    .then_inc(sem("f_rstd"), 1)

        @block.vector
        def _(dve):
            for t in range(NT):
                dve.wait_ge(sem("f_rstd"), t + 1)
                dve.scalar_tensor_tensor(x1[:, t], x1[:, t], f_rstd[:, t:t + 1], fin_gain[:], ALU.mult, ALU.mult) \
                    .then_inc(sem("out_ready"), 1)
    end_section()


_INS = ["x", "c", "ada_w", "ada_b", "norm_mix", "norm_ffn", "w_in", "gla_w_g2", "gla_b_g2", "gla_norm", "ml_i_bias",
        "ml_f_bias", "ml_norm", "gdn_conv", "gdn_a_log", "gdn_dt_bias", "gdn_norm", "w_out", "w_ffn_up", "w_ffn_down",
        "norm_final"]
_OUTS = [((1, S, D), "float32")]


def kernel(**inputs):
    import numpy as _np
    import concourse.bacc as _bacc
    from concourse import mybir as _mybir
    from concourse.bass_utils import run_bass_kernel_spmd as _run

    nc = _bacc.Bacc("TRN2", target_bir_lowering=False, num_devices=1)
    arrays, args = {}, []
    for name in _INS:
        a = _np.ascontiguousarray(inputs[name])
        arrays[f"in_{name}_dram"] = a
        args.append(nc.dram_tensor(f"in_{name}_dram", a.shape, _mybir.dt.from_np(a.dtype), kind="ExternalInput").ap())
    for i, (shape, dtype) in enumerate(_OUTS):
        dt = _mybir.dt.from_np(_np.dtype(dtype))
        args.append(nc.dram_tensor(f"out_{i}_dram", shape, dt, kind="ExternalOutput").ap())
    hybrid_block(nc, *args)
    r = _run(nc, [arrays], core_ids=[0])
    return r.results[0]["out_0_dram"]
```

```python
from contextlib import ExitStack

import concourse.bass as bass
from concourse import mybir

F32 = mybir.dt.float32
F32R = mybir.dt.float32r
ALU = mybir.AluOpType
ACT = mybir.ActivationFunctionType
ds = bass.ds

P = 128
D = 1024
S = 1024
EPS = 1e-6
KT = D // P
NT = S // P
GLA_H, GLA_DK, GLA_DV, GLA_RANK, GLA_GATE_NORM, SUB = 4, 128, 256, 16, 16.0, 16
ML_H, ML_DK, ML_DV, ML_CAP, ML_M_INIT = 4, 128, 256, 15.0, -1e30
GDN_H, GDN_DK, GDN_DV, GDN_TAPS = 8, 128, 128, 4
D_FF = 2816
NEG = -1e30
LN_DK = -2.4260151319598084

_SIZES = [512, 512, D, D, GLA_RANK, 512, 512, D, D, ML_H, ML_H, 3 * D, D, GDN_H, GDN_H, 3 * D]
_NAMES = ["gla_q", "gla_k", "gla_v", "gla_r", "gla_glr", "ml_q", "ml_k", "ml_v", "ml_o", "ml_i", "ml_f",
          "gdn_qkv", "gdn_z", "gdn_a", "gdn_b", "merge"]
COL = {n: sum(_SIZES[:i]) for i, n in enumerate(_NAMES)}
D_IN = sum(_SIZES)
SMALL = GLA_RANK + 2 * ML_H + 2 * GDN_H
LEVELS = [2, 4, 8, 16, 32, 64]
HALF = S // 2
MAX_SEMS = 120


class Count:

    def __init__(self, sem, step=1):
        self.sem, self.step, self.n = sem, step, 0

    def inc(self, ins):
        self.n += self.step
        ins.then_inc(self.sem, self.step)

    def wait(self, eng):
        if self.n:
            eng.wait_ge(self.sem, self.n)


def hybrid_block(nc, x, c, ada_w, ada_b, norm_mix, norm_ffn, w_in, gla_w_g2, gla_b_g2, gla_norm,
                 ml_i_bias, ml_f_bias, ml_norm, gdn_conv, gdn_a_log, gdn_dt_bias, gdn_norm,
                 w_out, w_ffn_up, w_ffn_down, norm_final, out):
    ctx = ExitStack()
    with ctx:
        _build(ctx, nc, x[0], c, ada_w[0], ada_b[0], norm_mix[0], norm_ffn[0], w_in[0], gla_w_g2[0], gla_b_g2[0],
               gla_norm[0], ml_i_bias[0], ml_f_bias[0], ml_norm[0], gdn_conv[0], gdn_a_log[0], gdn_dt_bias[0],
               gdn_norm[0], w_out[0], w_ffn_up[0], w_ffn_down[0], norm_final, out[0])


def _build(ctx, nc, x, c, ada_w, ada_b, norm_mix, norm_ffn, w_in, gla_w_g2, gla_b_g2, gla_norm,
           ml_i_bias, ml_f_bias, ml_norm, gdn_conv, gdn_a_log, gdn_dt_bias, gdn_norm,
           w_out, w_ffn_up, w_ffn_down, norm_final, out):

    def sb(name, shape, dt=F32, stack=ctx):
        return stack.enter_context(nc.sbuf_tensor(name, shape, dt))

    sems, cleared = {}, {}

    def sem(name):
        if name in cleared:
            sems[name] = cleared.pop(name)
        elif name not in sems:
            spare = len(sems) + len(cleared) < MAX_SEMS
            sems[name] = ctx.enter_context(nc.semaphore(name)) if spare else cleared.pop(next(iter(cleared)))
        return sems[name]

    def end_section():
        nc.all_engine_barrier()
        nums = sorted(s.num for s in sems.values())
        start = prev = nums[0]
        for n in nums[1:] + [None]:
            if n != prev + 1 if n is not None else True:
                nc.sync.sem_clear(range(start, prev + 1))
                start = n
            prev = n
        nc.all_engine_barrier()
        cleared.update(sems)
        sems.clear()

    banks = [ctx.enter_context(nc.psum_tensor(f"bank{i}", [P, 512], F32)) for i in range(8)]

    ident = sb("ident", [P, P])
    tri = sb("tri", [P, P])
    ones = sb("ones", [P, P])
    eps = sb("eps", [P, 1])
    ln_dk = sb("ln_dk", [P, 1])
    last_row = sb("last_row", [P, P])
    neg_mask = sb("neg_mask", [P, 2, P])
    level_mask = sb("level_mask", [P, len(LEVELS), 64])
    pair_mask = sb("pair_mask", [P, P])

    gates_dram = nc.dram_tensor("gates_scratch", (2, D), F32, kind="Internal").ap()
    y_dram = nc.dram_tensor("y_scratch", (3, S, D), F32, kind="Internal").ap()

    h_hi = sb("h_hi", [P, KT, S], F32R)
    h_lo = sb("h_lo", [P, KT, S], F32R)
    mod_col = sb("mod_col", [P, 4, KT])
    conv_col = sb("conv_col", [P, GDN_TAPS * 24])
    w_raw = sb("w_raw", [P, 2, KT, P])
    inproj = ExitStack()
    w_buf = {n: [sb(f"w{n}_{h}", [P, KT, w], F32R, stack=inproj if n == "C" else ctx) for h in ("hi", "lo")]
             for n, w in (("A", 256), ("B", 256), ("C", P))}

    A_W, B_W, C_W = (w_buf[n] for n in "ABC")

    with nc.Block() as block:
        @block.gpsimd
        def _(pool):
            made = Count(sem("const_made"))

            def fill(ap, v):
                made.inc(pool.memset(ap, v))

            fill(ident[:], 0.0)
            fill(tri[:], 1.0)
            fill(ones[:], 1.0)
            fill(eps[:], EPS)
            fill(ln_dk[:], LN_DK)
            fill(last_row[:], 1.0)
            fill(neg_mask[:], 0.0)
            fill(level_mask[:], 1.0)
            fill(pair_mask[:], 0.0)
            made.wait(pool)

            def select(ap, pattern, base, mult, op, value):
                made.inc(pool.affine_select(out=ap, in_=ap, pattern=pattern, base=base, channel_multiplier=mult,
                                            compare_op=op, fill=value))

            select(ident[:], [[-1, P]], 0, 1, ALU.not_equal, 1.0)
            select(tri[:], [[1, P]], 0, -1, ALU.is_ge, 0.0)
            select(last_row[:], [[0, P]], -(P - 1), 1, ALU.is_ge, 0.0)
            select(neg_mask[:, 0], [[1, P]], -1, -1, ALU.is_ge, NEG)
            select(neg_mask[:, 1], [[1, P]], 0, -1, ALU.is_ge, NEG)
            select(pair_mask[:].rearrange("p (n r) -> p n r", r=2)[:, :, 1], [[-2, P // 2]], 0, 1,
                   ALU.not_equal, -1.0)
            for v, b in enumerate(LEVELS):
                m = level_mask[:, v].rearrange("p (n b) -> p n b", b=b)
                select(m, [[-2 * b, 64 // b], [0, b]], -b, 1, ALU.is_ge, 0.0)
                made.wait(pool)
                select(m, [[2 * b, 64 // b], [0, b]], 2 * b - 1, -1, ALU.is_ge, 0.0)
            made.wait(pool)
    end_section()

    gdn_g = sb("gdn_g", [P, 4, NT, GDN_H], stack=inproj)
    ml_g = sb("ml_g", [P, 6, NT, ML_H], stack=inproj)
    glr_t = sb("glr_t", [GLA_RANK, S], stack=inproj)

    w_v = w_in.rearrange("(k p) n -> p k n", p=P)

    def load_half(sp, i, src):
        sp.dma_start(w_raw[:, i, :, 0:src.shape[2]], src).then_inc(sem(f"w_in{i}"), 16)

    def qk_cols(q0, k0):
        return [w_v[:, :, ds(q0, P)], w_v[:, :, ds(k0, P)]]

    def split(pool, i, buf, width, own, gate=None, gated=None):
        hi, lo = (w[:, :, i * width:(i + 1) * width] for w in buf)
        raw = w_raw[:, i, :, 0:width]
        if gate is not None:
            gated.inc(pool.tensor_tensor(raw, raw, gate.unsqueeze(1).broadcast_to([P, KT, width]), ALU.mult))
            gated.wait(pool)
        own.inc(pool.tensor_copy(hi, raw))
        own.wait(pool)
        own.inc(pool.tensor_tensor(lo, raw, hi.bitcast(F32), ALU.subtract))
        own.wait(pool)

    mod = ExitStack()
    ROWS = 48 + 3 * KT
    vec_rows = sb("vec_rows", [ROWS, P], stack=mod)
    vec_col = sb("vec_col", [P, ROWS], stack=mod)
    conv_rows = sb("conv_rows", [GDN_TAPS * 24, P], stack=mod)
    c_col = vec_col[:, 64:72]
    c_sig = sb("c_sig", [P, KT], stack=mod)
    c_act = sb("c_act", [P, KT], stack=mod)
    ada_b_col = vec_col[:, 0:48].rearrange("p (a k) -> p a k", k=KT)
    gain_col = vec_col[:, 48:64].rearrange("p (a k) -> p a k", k=KT)
    gate_row = sb("gate_row", [1, 2, D], stack=mod)
    ADA_W, ADA_SLOTS = 256, 4
    ada_ring = sb("ada_ring", [P, ADA_SLOTS, KT, ADA_W], stack=mod)
    ada_v = ada_w.rearrange("(k p) n -> p k n", p=P)
    ADA = [(part, j) for part in (0, 1, 2, 3, 4, 5) for j in range(D // ADA_W)]

    def ada_load(sp, m, m0):
        part, j = ADA[m]
        if m - m0 >= ADA_SLOTS:
            sp.wait_ge(sem("ada_up"), m - m0 - ADA_SLOTS + 1)
        o = part * D + j * ADA_W
        sp.dma_start(ada_ring[:, (m - m0) % ADA_SLOTS], ada_v[:, :, o:o + ADA_W]) \
            .then_inc(sem(f"ada_in{(m - m0) % ADA_SLOTS}"), 16)

    def ada_pe(pe, m, m0):
        part, j = ADA[m]
        slot, bank = (m - m0) % ADA_SLOTS, banks[6 + (m - m0) % 2]
        pe.wait_ge(sem(f"ada_in{slot}"), 16 * ((m - m0) // ADA_SLOTS + 1))
        if m - m0 >= 2:
            pe.wait_ge(sem("ada_out"), m - m0 - 1)
        if part % 3 == 2:
            for k in range(KT):
                mm = nc.tensor.matmul(bank[0:1, 0:ADA_W], c_act[:, k:k + 1], ada_ring[:, slot, k], start=(k == 0),
                                      stop=(k == KT - 1))
        else:
            for i in range(ADA_W // P):
                for k in range(KT):
                    mm = nc.tensor.matmul(bank[:, i:i + 1], ada_ring[:, slot, k, i * P:i * P + P], c_act[:, k:k + 1],
                                          start=(k == 0), stop=(k == KT - 1))
        mm.then_inc(sem("ada_up"), 1)

    def ada_dve(dve, m, m0):
        part, j = ADA[m]
        bank = banks[6 + (m - m0) % 2]
        dve.wait_ge(sem("ada_up"), m - m0 + 1)
        n = ADA_W // P
        cols = slice(n * j, n * j + n)
        if part % 3 == 2:
            g = gate_row[:, part // 3, j * ADA_W:(j + 1) * ADA_W]
            dve.tensor_tensor(g, g, bank[0:1, 0:ADA_W], ALU.add).then_inc(sem("ada_out"), 1)
        elif part % 3 == 0:
            dve.tensor_tensor(mod_col[:, 2 * (part // 3) + 1, cols], bank[:, 0:n], ada_b_col[:, part, cols], ALU.add) \
                .then_inc(sem("ada_out"), 1)
        else:
            dst = mod_col[:, 2 * (part // 3), cols]
            dve.scalar_tensor_tensor(dst, bank[:, 0:n], 1.0, ada_b_col[:, part, cols], ALU.add, ALU.add) \
                .then_inc(sem("ada_out"), 1)
            dve.wait_ge(sem("ada_out"), m - m0 + 1)
            dve.tensor_tensor(dst, dst, gain_col[:, part // 3, cols], ALU.mult).then_inc(sem("ada_scale"), 1)

    ADA_SPLIT = (0, 8, 12, 24)
    pro = ExitStack()
    x_rows = sb("x_rows", [P, NT, D], stack=pro)
    with nc.Block() as block:
        @block.sync
        def _(sp):
            for lo, n, v in ((0, 48, ada_b), (48, 8, norm_mix), (56, 8, norm_ffn), (64, 8, c[0])):
                sp.dma_start(vec_rows[lo:lo + n, :], v.rearrange("(k p) -> k p", p=P)).then_inc(sem("vec_in"), 16)
            sp.dma_start(conv_rows[:], gdn_conv.rearrange("j (k p) -> (j k) p", p=P)).then_inc(sem("vec_in"), 16)
            for m in range(4):
                ada_load(sp, m, 0)
            for o, name, n in ((0, "gla_glr", 16), (16, "ml_i", 8), (24, "gdn_a", 16)):
                sp.dma_start(w_raw[:, 0, :, o:o + n], w_v[:, :, COL[name]:COL[name] + n]).then_inc(sem("w_small"), 16)
            for i in range(2):
                sp.dma_start(gate_row[:, i], ada_b[(3 * i + 2) * D:(3 * i + 3) * D].unsqueeze(0)) \
                    .then_inc(sem("row_in"), 16)
            for m in range(4, ADA_SPLIT[1]):
                ada_load(sp, m, 0)
            sp.wait_ge(sem("row_in"), 32)

        @block.gpsimd
        def _(pool):
            pool.wait_ge(sem("w_small"), 48)
            split(pool, 0, C_W, SMALL, Count(sem("w_split")))

        @block.scalar
        def _(act):
            act.wait_ge(sem("cols_up"), 2)
            nc.scalar.activation(vec_col[:], banks[5][:, 0:ROWS], ACT.Copy).then_inc(sem("cols"), 1)
            nc.scalar.activation(conv_col[:], banks[4][:, 0:GDN_TAPS * 24], ACT.Copy).then_inc(sem("cols"), 1)
            act.wait_ge(sem("cols"), 2)
            nc.scalar.activation(c_sig[:], c_col, ACT.Exp, scale=-1.0).then_inc(sem("c_exp"), 1)

        @block.vector
        def _(dve):
            done = Count(sem("c_act"))
            dve.wait_ge(sem("c_exp"), 1)
            done.inc(dve.tensor_scalar(c_sig[:], c_sig[:], 1.0, None, ALU.add))
            done.wait(dve)
            done.inc(dve.reciprocal(c_sig[:], c_sig[:]))
            done.wait(dve)
            done.inc(dve.tensor_tensor(c_act[:], c_col, c_sig[:], ALU.mult))
            for m in range(ADA_SPLIT[1]):
                ada_dve(dve, m, 0)

        @block.tensor
        def _(pe):
            pe.wait_ge(sem("vec_in"), 80)
            nc.tensor.transpose(banks[5][:, 0:ROWS], vec_rows[:], ident[0:ROWS, 0:ROWS]).then_inc(sem("cols_up"), 1)
            nc.tensor.transpose(banks[4][:, 0:GDN_TAPS * 24], conv_rows[:], ident[0:96, 0:96]) \
                .then_inc(sem("cols_up"), 1)
            pe.wait_ge(sem("c_act"), 3)
            for m in range(ADA_SPLIT[1]):
                ada_pe(pe, m, 0)
    end_section()

    def norm_to_feature_major(rows, load, ada, weights):
        st = ExitStack()
        full = sb("tf_full", [P, 2, 512], stack=st)
        junk = sb("tf_junk", [P, D], stack=st)
        ss = sb("tf_ss", [P, NT], stack=st)
        rstd = sb("tf_rstd", [P, NT], stack=st)
        with nc.Block() as block:
            @block.sync
            def _(sp):
                for t in range(NT):
                    sp.dma_start(rows[:, t], load[t * P:t * P + P, :]).then_inc(sem(f"rows_in{t}"), 16)
                for i, w in enumerate(weights):
                    load_half(sp, i, w)
                for m in range(*ada):
                    ada_load(sp, m, ada[0])

            @block.gpsimd
            def _(pool):
                own = Count(sem("w_split"))
                for i, _ in enumerate(weights):
                    pool.wait_ge(sem(f"w_in{i}"), 16)
                    split(pool, i, A_W, P, own)

            @block.scalar
            def _(act):
                nc.scalar.preload_act_table_set("natural_log_exp_and_others")
                rms = Count(sem("tf_ln"))
                for t in range(NT):
                    act.wait_ge(sem(f"rows_in{t}"), 16)
                    if t:
                        act.wait_ge(sem("tf_square"), t)
                    nc.scalar.activation(junk[:], rows[:, t], ACT.Square, accum_out=ss[:, t:t + 1]) \
                        .then_inc(sem("tf_square"), 1)
                    act.wait_ge(sem("tf_square"), t + 1)
                    rms.inc(nc.scalar.activation(ss[:, t:t + 1], ss[:, t:t + 1], ACT.Ln, scale=1.0 / D, bias=eps[:]))
                    rms.wait(act)
                    nc.scalar.activation(rstd[:, t:t + 1], ss[:, t:t + 1], ACT.Exp, scale=-0.5) \
                        .then_inc(sem("tf_rstd"), 1)
                for n in range(2 * KT):
                    act.wait_ge(sem("tf_full"), n + 1)
                    k, half = n % KT, n // KT
                    nc.scalar.activation(h_hi[:, k, half * 512:half * 512 + 512], full[:, n % 2], ACT.Copy) \
                        .then_inc(sem("tf_hi"), 1)

            @block.vector
            def _(dve):
                for t in range(NT):
                    dve.wait_ge(sem("tf_rstd"), t + 1)
                    dve.tensor_scalar(rows[:, t], rows[:, t], rstd[:, t:t + 1], None, ALU.mult) \
                        .then_inc(sem("tf_rows"), 1)
                for n in range(2 * KT):
                    k, half = n % KT, n // KT
                    dve.wait_ge(sem("tf_up"), n + 1)
                    if n >= 2:
                        dve.wait_ge(sem("tf_lo"), n - 1)
                    b = banks[n % 4][:]
                    dve.tensor_scalar(full[:, n % 2], b, mod_col[:, 0, k:k + 1], mod_col[:, 1, k:k + 1], ALU.mult,
                                      ALU.add).then_inc(sem("tf_full"), 1)
                    dve.wait_ge(sem("tf_hi"), n + 1)
                    dve.tensor_tensor(h_lo[:, k, half * 512:half * 512 + 512], full[:, n % 2],
                                      h_hi[:, k, half * 512:half * 512 + 512].bitcast(F32), ALU.subtract) \
                        .then_inc(sem("tf_lo"), 1)
                for m in range(*ada):
                    ada_dve(dve, m, ada[0])

            @block.tensor
            def _(pe):
                for n in range(2 * KT):
                    k, half = n % KT, n // KT
                    pe.wait_ge(sem("tf_rows"), 4 * half + 4)
                    if n >= 4:
                        pe.wait_ge(sem("tf_full"), n - 3)
                    for j in range(4):
                        tp = nc.tensor.transpose(banks[n % 4][:, j * P:j * P + P],
                                                 rows[:, 4 * half + j, k * P:k * P + P], ident[:])
                    tp.then_inc(sem("tf_up"), 1)
                for m in range(*ada):
                    ada_pe(pe, m, ada[0])
        end_section()
        st.close()

    norm_to_feature_major(x_rows, x, ADA_SPLIT[1:3], qk_cols(COL["gdn_qkv"], COL["gdn_qkv"] + D))
    pro.close()

    PASSES = [(0, 0), (0, 1), (1, 0)]

    def token_major(bank, t, buf, n0, n1, steps, n_out=0):
        for s in steps:
            k, (wp, hp) = s // 3, PASSES[s % 3]
            mm = nc.tensor.matmul(bank[:, n_out:n_out + n1 - n0], (h_hi, h_lo)[hp][:, k, t * P:t * P + P],
                                  buf[wp][:, k, n0:n1], start=(s == 0), stop=(s == 3 * KT - 1))
        return mm

    def feature_major(bank, half, buf, n0, steps, n=P):
        for s in steps:
            k, (wp, hp) = s // 3, PASSES[s % 3]
            mm = nc.tensor.matmul(bank[0:n, :], buf[wp][:, k, n0:n0 + n],
                                  (h_hi, h_lo)[hp][:, k, half * HALF:half * HALF + HALF],
                                  start=(s == 0), stop=(s == 3 * KT - 1))
        return mm

    gt = ExitStack()
    pf = sb("pf", [SMALL, S], stack=gt)
    pg = sb("pg", [P, NT, SMALL], stack=gt)
    gb = sb("gb", [P, 2 * ML_H + 2 * GDN_H], stack=gt)
    u1 = sb("u1", [P, NT, 16], stack=gt)
    u2 = sb("u2", [P, NT, 16], stack=gt)
    u3 = sb("u3", [P, NT, 16], stack=gt)
    rate = sb("rate", [P, GDN_H], stack=gt)
    capped = sb("capped", [P, NT, 2 * ML_H], stack=gt)
    mt1 = sb("mt1", [P, NT, 2 * ML_H], stack=gt)
    logs = sb("logs", [P, NT * (GDN_H + ML_H)], stack=gt)
    cums = sb("cums", [P, NT * (GDN_H + ML_H)], stack=gt)
    tots = sb("tots", [P, NT * (GDN_H + ML_H)], stack=gt)
    rows = sb("rows", [ML_H, 3, S], stack=gt)
    m_col = sb("m_col", [P, NT, ML_H], stack=gt)
    m_end = sb("m_end", [P, NT, ML_H], stack=gt)
    mx = sb("mx", [P, 3, NT, ML_H], stack=gt)
    NG, NM = NT * GDN_H, NT * ML_H
    ROW_BANKS = ((1, 2), (5, 0))
    ADA_AT = (1, 2, 2, 1)
    logs_g = logs[:, 0:NG].rearrange("p (t h) -> p t h", h=GDN_H)
    logs_m = logs[:, NG:].rearrange("p (t h) -> p t h", h=ML_H)
    cum_g = cums[:, 0:NG].rearrange("p (t h) -> p t h", h=GDN_H)
    cum_m = cums[:, NG:].rearrange("p (t h) -> p t h", h=ML_H)
    tot_g = tots[:, 0:NG].rearrange("p (t h) -> p t h", h=GDN_H)
    tot_m = tots[:, NG:].rearrange("p (t h) -> p t h", h=ML_H)

    def over_tiles(row):
        n = row.shape[1]
        return row.unsqueeze(1).broadcast_to([P, NT, n])

    with nc.Block() as block:
        @block.sync
        def _(sp):
            for o, v in ((0, ml_i_bias), (4, ml_f_bias), (8, gdn_dt_bias), (16, gdn_a_log)):
                sp.dma_start(gb[:, o:o + v.shape[0]], v.partition_broadcast(P)).then_inc(sem("bias_in"), 16)
            m0, m1 = ADA_SPLIT[2:4]
            for m in range(m0, m1):
                ada_load(sp, m, m0)
            sp.wait_ge(sem("ada_out"), m1 - m0)
            sp.dma_start(gates_dram.unsqueeze(0), gate_row[:]).then_inc(sem("gates_out"), 16)
            sp.wait_ge(sem("gates_out"), 16)

        @block.tensor
        def _(pe):
            for half in range(2):
                feature_major(banks[1 + half], half, C_W, 0, range(3 * KT), SMALL).then_inc(sem("pf_up"), 1)
            pe.wait_ge(sem("pf"), 2)
            for t in range(NT):
                tp = nc.tensor.transpose(banks[0][:, t * SMALL:(t + 1) * SMALL], pf[:, t * P:t * P + P],
                                         ident[0:SMALL, 0:SMALL])
            tp.then_inc(sem("pg_up"), 1)
            ada = iter(range(*ADA_SPLIT[2:4]))

            def some_ada(n):
                for _ in range(n):
                    ada_pe(pe, next(ada), ADA_SPLIT[2])

            some_ada(ADA_AT[0])
            some_ada(ADA_AT[1])
            pe.wait_ge(sem("logs"), 1)
            nc.tensor.matmul(banks[3][:, 0:NG + NM], tri[:], logs[:], start=True, stop=True).then_inc(sem("cum_up"), 1)
            nc.tensor.matmul(banks[4][:, 0:NG + NM], ones[:], logs[:], start=True, stop=True).then_inc(sem("cum_up"), 1)
            pe.wait_ge(sem("glr"), 2)
            for q in range(2):
                for t in range(NT):
                    src = logs_m[:, t] if q == 0 else capped[:, t, 0:ML_H]
                    bank = banks[ROW_BANKS[q][t // 4]]
                    tp = nc.tensor.transpose(bank[0:ML_H, t % 4 * P:t % 4 * P + P], src, ident[:])
            tp.then_inc(sem("rows_up"), 1)
            some_ada(ADA_AT[2])
            pe.wait_ge(sem("m_row"), 1)
            for t in range(NT):
                tp = nc.tensor.transpose(banks[0][:, t * ML_H:(t + 1) * ML_H], rows[:, 2, t * P:t * P + P],
                                         ident[0:ML_H, 0:ML_H])
            tp.then_inc(sem("m_up"), 1)
            some_ada(ADA_AT[3])
            pe.wait_ge(sem("m_col"), 1)
            nc.tensor.matmul(banks[3][:, 0:NM], last_row[:], m_col[:].rearrange("p t h -> p (t h)"), start=True,
                             stop=True).then_inc(sem("m_end_up"), 1)
            for m in ada:
                ada_pe(pe, m, ADA_SPLIT[2])

        @block.scalar
        def _(act):
            A = nc.scalar.activation
            own = Count(sem("gate_act"))
            nc.scalar.preload_act_table_set("natural_log_exp_and_others")
            act.wait_ge(sem("bias_in"), 64)
            own.inc(A(rate[:], gb[:, 16:24], ACT.Exp))
            for h in range(2):
                act.wait_ge(sem("pf_up"), h + 1)
                A(pf[:, h * HALF:(h + 1) * HALF], banks[1 + h][0:SMALL, :], ACT.Copy).then_inc(sem("pf"), 1)
                A(glr_t[:, h * HALF:(h + 1) * HALF], banks[1 + h][0:GLA_RANK, :], ACT.Copy).then_inc(sem("glr"), 1)
            act.wait_ge(sem("pre_cap"), 1)
            own.inc(A(capped[:], capped[:], ACT.Tanh, scale=1.0 / ML_CAP))
            act.wait_ge(sem("pre_exp"), 2)
            own.inc(A(u2[:], u2[:], ACT.Abs))
            own.wait(act)
            own.inc(A(u2[:], u2[:], ACT.Exp, scale=-1.0))
            own.inc(A(mt1[:, :, ML_H:], capped[:, :, ML_H:], ACT.Exp, scale=-1.0))
            own.wait(act)
            own.inc(A(u2[:], u2[:], ACT.Ln, bias=1.0))
            own.inc(A(mt1[:, :, ML_H:], mt1[:, :, ML_H:], ACT.Ln, bias=1.0))
            act.wait_ge(sem("ln_beta"), 1)
            own.inc(A(gdn_g[:, 2], gdn_g[:, 1], ACT.Exp))
            act.wait_ge(sem("rows_up"), 1)
            for q in range(2):
                for h in range(2):
                    own.inc(A(rows[:, q, h * HALF:(h + 1) * HALF], banks[ROW_BANKS[q][h]][0:ML_H, :], ACT.Copy))
            act.wait_ge(sem("ml_exps"), 1)
            own.inc(A(ml_g[:, 3:6], mx[:], ACT.Exp))

        @block.vector
        def _(dve):
            own = Count(sem("gate_dve"))
            dve.wait_ge(sem("pg_up"), 1)
            dve.tensor_copy(pg[:].rearrange("p t n -> p (t n)"), banks[0][:, 0:NT * SMALL]).then_inc(sem("pg"), 1)
            dve.wait_ge(sem("pg"), 1)
            ada = iter(range(*ADA_SPLIT[2:4]))

            def some_ada(n):
                for _ in range(n):
                    ada_dve(dve, next(ada), ADA_SPLIT[2])

            dve.wait_ge(sem("bias_in"), 64)
            dve.tensor_tensor(capped[:], pg[:, :, 16:24], over_tiles(gb[:, 0:8]), ALU.add).then_inc(sem("pre_cap"), 1)
            own.inc(dve.tensor_tensor(u1[:, :, 0:8], pg[:, :, 24:32], over_tiles(gb[:, 8:16]), ALU.add))
            own.inc(dve.tensor_scalar(u1[:, :, 8:16], pg[:, :, 32:40], -1.0, None, ALU.mult))
            own.wait(dve)
            dve.tensor_copy(u2[:], u1[:]).then_inc(sem("pre_exp"), 1)
            own.inc(dve.tensor_scalar(u3[:], u1[:], 0.0, None, ALU.max))
            some_ada(ADA_AT[0])
            dve.wait_ge(sem("gate_act"), 2)
            dve.tensor_scalar(capped[:], capped[:], ML_CAP, None, ALU.mult).then_inc(sem("pre_exp"), 1)
            dve.wait_ge(sem("gate_act"), 7)
            own.inc(dve.tensor_tensor(u3[:], u3[:], u2[:], ALU.add))
            own.wait(dve)
            dve.tensor_scalar(gdn_g[:, 1], u3[:, :, 8:16], -1.0, None, ALU.mult).then_inc(sem("ln_beta"), 1)
            own.inc(dve.scalar_tensor_tensor(logs_g, u3[:, :, 0:8], -1.0, over_tiles(rate[:]), ALU.mult, ALU.mult))
            dve.tensor_scalar(logs_m, mt1[:, :, ML_H:], -1.0, None, ALU.mult).then_inc(sem("logs_m"), 1)
            dve.wait_ge(sem("logs_m"), 1)
            own.wait(dve)
            dve.tensor_copy(m_end[:], logs_m).then_inc(sem("logs"), 1)
            some_ada(ADA_AT[1])
            dve.wait_ge(sem("cum_up"), 2)
            own.inc(dve.tensor_copy(cums[:], banks[3][:, 0:NG + NM]))
            own.inc(dve.tensor_copy(tots[:], banks[4][:, 0:NG + NM]))
            own.wait(dve)
            own.inc(dve.tensor_copy(gdn_g[:, 0], cum_g))
            own.inc(dve.tensor_copy(gdn_g[:, 3], tot_g))
            some_ada(ADA_AT[2])
            dve.wait_ge(sem("gate_act"), 12)
            dve.tensor_tensor_scan(rows[:, 2], rows[:, 0], rows[:, 1], ML_M_INIT, ALU.add, ALU.max) \
                .then_inc(sem("m_row"), 1)
            dve.wait_ge(sem("m_up"), 1)
            dve.tensor_copy(m_col[:], banks[0][:, 0:NM].rearrange("p (t h) -> p t h", h=ML_H)).then_inc(sem("m_col"), 1)
            some_ada(ADA_AT[3])
            dve.wait_ge(sem("m_col"), 1)
            dve.wait_ge(sem("m_end_up"), 1)
            own.inc(dve.tensor_copy(m_end[:], banks[3][:, 0:NM].rearrange("p (t h) -> p t h", h=ML_H)))
            own.inc(dve.memset(ml_g[:, 2, 0], ML_M_INIT))
            own.inc(dve.scalar_tensor_tensor(ml_g[:, 0], m_col[:], -1.0, cum_m, ALU.mult, ALU.add))
            own.inc(dve.tensor_tensor(ml_g[:, 1], capped[:, :, 0:ML_H], cum_m, ALU.subtract))
            own.wait(dve)
            own.inc(dve.tensor_copy(ml_g[:, 2, 1:NT], m_end[:, 0:NT - 1]))
            own.inc(dve.tensor_tensor(mx[:, 0], tot_m, m_end[:], ALU.subtract))
            own.inc(dve.tensor_scalar(mx[:, 2], m_col[:], -1.0, None, ALU.mult))
            own.wait(dve)
            own.inc(dve.tensor_scalar(ml_g[:, 0], ml_g[:, 0], LN_DK, None, ALU.add))
            own.inc(dve.tensor_tensor(mx[:, 1], mx[:, 0], ml_g[:, 2], ALU.add))
            own.wait(dve)
            dve.tensor_tensor(mx[:, 0], mx[:, 0], ml_g[:, 1], ALU.add).then_inc(sem("ml_exps"), 1)
            for m in ada:
                ada_dve(dve, m, ADA_SPLIT[2])
    end_section()
    gt.close()
    mod.close()

    mixers = ExitStack()

    def mb(name, shape, dt=F32):
        return sb(name, shape, dt, stack=mixers)

    kq = mb("kq", [P, 2, S])
    v_t = mb("v_t", [P, S])
    gdn_m = mb("gdn_m", [P, NT, GDN_DV])
    conv_in = mb("conv_in", [P, 2, S + GDN_TAPS - 1])
    pair_buf = mb("pair_buf", [P, 20 * P])
    conv_acc = pair_buf[:, 12 * P:20 * P]
    gh = mb("gh", [P, 4, NT])
    conv_w = mb("conv_w", [P, GDN_TAPS, 3])
    lnss = mb("lnss", [P, 2, NT])
    gq = mb("gq", [P, 4, NT])
    gex = mb("gex", [P, 3, NT])
    qg = mb("qg", [P, S])
    kg = mb("kg", [P, S])
    vg = mb("vg", [P, NT, GLA_DV + 1])
    mg = mb("mg", [P, NT, GLA_DV])
    sig = mb("sig", [P, 2, 256])
    gain_g = mb("gain_g", [P, 2, GLA_DV])
    gain_d = mb("gain_d", [P, GDN_DV])
    wts = pair_buf[:, 0 * P:4 * P].rearrange("p (c n) -> p c n", c=2)
    at = pair_buf[:, 4 * P:8 * P].rearrange("p (c n) -> p c n", c=2)
    qdec = pair_buf[:, 12 * P:14 * P].rearrange("p (c n) -> p c n", c=2)
    xm = pair_buf[:, 8 * P:10 * P].rearrange("p (c n) -> p c n", c=2)
    xmt = pair_buf[:, 10 * P:12 * P].rearrange("p (c n) -> p c n", c=2)
    pm = mb("pm", [P, len(LEVELS), 2, P])
    kend = pair_buf[:, 14 * P:16 * P].rearrange("p (c n) -> p c n", c=2)
    vbeta = pair_buf[:, 16 * P:18 * P].rearrange("p (c n) -> p c n", c=2)
    rhs = pair_buf[:, 18 * P:19 * P]
    vnew = pair_buf[:, 19 * P:20 * P]
    state_d = mb("state_d", [P, P])
    junk = mb("junk", [P, 256])
    ybuf = mb("ybuf", [P, 2, 256])
    rs = mb("rs", [P, 4])
    w_g2 = mb("w_g2", [GLA_RANK, P])
    b_g2 = mb("b_g2", [P, 1])
    la = pair_buf[:, 0 * P:8 * P]
    gabs = pair_buf[:, 8 * P:12 * P]
    cum = mb("cum", [P, P])
    edge = mb("edge", [P, 2, NT])
    last16 = mb("last16", [P, 1])
    dl_col = mb("dl_col", [P, NT])
    dq = mb("dq", [P, P])
    ke = mb("ke", [P, P])
    kt_sub = mb("kt_sub", [P, NT, P])
    qd = mb("qd", [P, 2, P])
    sc = mb("sc", [P, P])
    kend_g = mb("kend_g", [P, P])
    state_g = mb("state_g", [P, GLA_DV + 1])
    mh = mb("mh", [P, 6, NT])

    G = banks[0:2]
    M = banks[2:8]

    class Steps:

        def __init__(self, eng, own):
            self.eng, self.own, self.counts = eng, own, {}

        def __call__(self, ins, name=None):
            n = self.counts.setdefault(name or self.own, Count(sem(name or self.own)))
            n.inc(ins)
            n.wait(self.eng)

        def free_bank(self, ins, u):
            ins.then_inc(sem(f"proj_read{u % 2}"), 1)
            self.eng.wait_ge(sem(f"proj_read{u % 2}"), u // 2 + 1)

    def gla_cols(br, f):
        q, k, v, r = (COL[n] for n in (("gla_q", "gla_k", "gla_v", "gla_r") if br == "gla" else
                                       ("ml_q", "ml_k", "ml_v", "ml_o")))
        g = COL["merge"] + (0 if br == "gla" else D)
        return [qk_cols(f * P + q, f * P + k)] + \
            [qk_cols(f * 256 + v, f * 256 + (v + P))] + \
            [qk_cols(f * 256 + (r + o), f * 256 + (g + o)) for o in (0, P)]

    def gdn_cols(h):
        o = COL["gdn_qkv"]
        return [qk_cols(h * P + o, h * P + (o + D)),
                [w_v[:, :, ds(h * P + (o + 2 * D + i), 64)] for i in (0, 64)],
                qk_cols(h * P + COL["gdn_z"], h * P + (COL["merge"] + 2 * D))]

    def gather_sp(sp, n, k, parts):
        if n >= 2:
            sp.wait_ge(sem("gather_up"), n - 1)
        for b in range(3):
            sp.dma_start(parts[n % 2][b], y_dram[b, :, k * P:k * P + P].rearrange("(t p) n -> p t n", p=P)) \
                .then_inc(sem(f"gather_in{n % 2}"), 16)

    def gather_sum(dve, n, parts):
        a, b, c = parts[n % 2]
        dve.wait_ge(sem(f"gather_in{n % 2}"), 48 * (n // 2 + 1))
        dve.tensor_tensor(a, a, b, ALU.add).then_inc(sem("gather_two"), 1)
        dve.wait_ge(sem("gather_two"), n + 1)
        dve.tensor_tensor(a, a, c, ALU.add).then_inc(sem("gather_sum"), 1)

    def gather_pe(pe, n, parts):
        pe.wait_ge(sem("gather_sum"), n + 1)
        if n:
            pe.wait_ge(sem("gather_lo"), 2 * n)
        for t in range(NT):
            tp = nc.tensor.transpose(banks[t // 4][:, t % 4 * P:t % 4 * P + P], parts[n % 2][0][:, t], ident[:])
        tp.then_inc(sem("gather_up"), 1)

    def gather_hi(act, n, k):
        act.wait_ge(sem("gather_up"), n + 1)
        for half in range(2):
            nc.scalar.activation(h_hi[:, k, half * HALF:(half + 1) * HALF], banks[half][:], ACT.Copy) \
                .then_inc(sem("gather_hi"), 1)

    def gather_lo(dve, n, k):
        for half in range(2):
            cols = slice(half * HALF, (half + 1) * HALF)
            dve.wait_ge(sem("gather_hi"), 2 * n + half + 1)
            dve.tensor_tensor(h_lo[:, k, cols], banks[half][:], h_hi[:, k, cols].bitcast(F32), ALU.subtract) \
                .then_inc(sem("gather_lo"), 1)

    def by_tile(ap):
        return ap.rearrange("p (t n) -> p t n", n=P)

    EARLY = 6
    early_parts = [(by_tile(conv_in[:, 0, 0:S]), by_tile(conv_in[:, 1, 0:S]), w_raw[:, 0]),
                   (by_tile(kq[:, 0]), by_tile(kq[:, 1]), by_tile(v_t[:]))]
    EARLY_AT = [3 + 7 * n for n in range(EARLY)]
    out_v = w_out.rearrange("(k p) n -> p k n", p=P)
    W_EARLY = 4
    W_EARLY_AT = [2 + 8 * m for m in range(W_EARLY)]


    BEATS1, CHUNK2 = 20, 5
    U1 = 28

    def mixer_section(br, f, h, next_h, prefetch):
        last = next_h is None
        PRE2 = 2 if br == "ml" else 6
        groups = []
        units = []

        def add_units(g, kind, span):
            units.extend((g, kind, i) for i in span)

        if br:
            groups += [(n, s, 256) for n, s in zip("ABAB", gla_cols(br, f))]
            for g, (kind, n) in enumerate((("qk", 4), ("v", NT), ("rg", NT), ("rg", NT))):
                add_units(g, kind, range(n))
        u0, g0 = len(units), len(groups)
        if next_h is not None:
            qk, v, zg = gdn_cols(next_h)
            groups += [("A", qk, 256), ("B", zg, 256), ("C", v, P)]
            add_units(g0, "gqk", range(4))
            add_units(g0 + 1, "zg", range(4))
            add_units(g0 + 2, "gv", range(2))
            add_units(g0 + 1, "zg", range(4, NT))
        n_units = len(units)
        if prefetch is not None:
            groups.append(("A", prefetch, 256))
        first_unit = {g: min(u for u in range(n_units) if units[u][0] == g) for g, _, _ in units}
        last_unit = {g: max(u for u in range(n_units) if units[u][0] == g) for g, _, _ in units}

        def gate_units(u):
            return sum(units[j][1] in ("rg", "zg") for j in range(u))

        def piece(pe, n):
            u, part = divmod(n, 3)
            g, kind, i = units[u]
            if part == 0:
                if first_unit[g] == u and g:
                    pe.wait_ge(sem("w_split"), 4 * g)
                if u >= 2:
                    pe.wait_ge(sem(f"proj_read{u % 2}"), u // 2)
            steps = range(8 * part, 8 * part + 8)
            buf = w_buf[groups[g][0]]
            if kind in ("qk", "gqk", "gv"):
                mm = feature_major(G[u % 2], i % 2, buf, (i // 2) * P, steps)
            else:
                mm = token_major(G[u % 2], i, buf, 0, 256, steps)
            if part == 2:
                mm.then_inc(sem(f"proj{u % 2}"), 1)

        def proj_ready(eng, u):
            eng.wait_ge(sem(f"proj{u % 2}"), u // 2 + 1)

        def act_unit(act, step, u):
            if not 0 <= u < n_units:
                return
            _, kind, i = units[u]
            b = G[u % 2]
            A = nc.scalar.activation
            proj_ready(act, u)
            half = (i % 2) * HALF
            if kind == "qk":
                step.free_bank(A((qg, kg)[i // 2][:, half:half + HALF], b[:], ACT.Copy), u)
            elif kind == "gqk":
                o = GDN_TAPS - 1 + half
                step.free_bank(A(conv_in[:, i // 2 % 2, o:o + HALF], b[:], ACT.Copy), u)
            elif kind == "gv":
                o = GDN_TAPS - 1 + half
                act.wait_ge(sem("conv_ss"), 1)
                step.free_bank(A(conv_in[:, 0, o:o + HALF], b[:], ACT.Copy), u)
            elif kind == "v":
                step.free_bank(A(vg[:, i, 0:GLA_DV], b[:, 0:256], ACT.Copy), u)
            else:
                n = gate_units(u)
                if n >= 2:
                    act.wait_ge(sem("sig_used"), n - 1)
                step(A(sig[:, n % 2], b[:, 0:256], ACT.Exp, scale=-1.0), "sig_exp")

        def dve_unit(dve, step, u, stage):
            if not 0 <= u < n_units:
                return
            g, kind, i = units[u]
            if kind not in ("rg", "zg"):
                return
            n = gate_units(u)
            ex, eg = sig[:, n % 2, 0:P], sig[:, n % 2, P:2 * P]
            j = g % 2 if br else 0
            if kind == "zg":
                factor, gain = gdn_m[:, i], gain_d[:]
            else:
                factor = mg[:, i, j * P:j * P + P]
                gain = gain_g[:, 0 if br == "gla" else 1, j * P:j * P + P]
            if stage == 0:
                dve.wait_ge(sem("sig_exp"), n + 1)
                if kind == "rg" and br == "ml":
                    step.free_bank(dve.tensor_copy(factor, gain), u)
                else:
                    step.free_bank(dve.tensor_tensor(factor, G[u % 2][:, 0:P], gain, ALU.mult), u)
                step(dve.tensor_scalar(eg, eg, 1.0, None, ALU.add))
                step(dve.scalar_tensor_tensor(ex, ex, 1.0, eg, ALU.add, ALU.mult))
            elif stage == 1:
                step(dve.reciprocal(ex, ex), "sig_recip")
            elif u < u0:
                finish_factor(dve, n, factor, ex)

        def finish_factor(eng, n, factor, ex):
            eng.wait_ge(sem("sig_recip"), n + 1)
            eng.tensor_tensor(factor, factor, ex, ALU.mult).then_inc(sem("sig_used"), 1)
            eng.wait_ge(sem("sig_used"), n + 1)

        def pool_unit(pool, u):
            if units[u][1] == "zg":
                n = gate_units(u)
                finish_factor(pool, n, gdn_m[:, units[u][2]], sig[:, n % 2, 0:P])

        def pair(ap, b, r):
            return ap.rearrange("p c (n r b) -> p c n r b", r=2, b=b)[:, :, :, r, :]

        def one(ap, b, r):
            return ap.rearrange("p (n r b) -> p n r b", r=2, b=b)[:, :, r, :]

        def gdn_front_pe(pe, d, part):
            mm = nc.tensor.matmul
            if part == 0:
                if d:
                    pe.wait_ge(sem("gdn_at"), d)
                for c in range(2):
                    t = (2 * d + c) * P
                    last = mm(M[0][:, c * 256:c * 256 + 256], kq[:, 0, t:t + P], kq[:, :, t:t + P], start=True,
                              stop=True)
                last.then_inc(sem("gdn_kq"), 1)
            elif part == 1:
                if d:
                    pe.wait_ge(sem("gdn_eq"), d)
                for c in range(2):
                    for q in range(2):
                        last = mm(M[1][:, (2 * c + q) * P:(2 * c + q + 1) * P],
                                  gq[:, q, 2 * d + c:2 * d + c + 1].broadcast_to([P, P]), ident[:], start=True,
                                  stop=True)
                last.then_inc(sem("gdn_row"), 1)
            else:
                if d:
                    pe.wait_ge(sem("gdn_kv"), d)
                for i, src in enumerate((kq[:, 0], v_t[:])):
                    for c in range(2):
                        t = (2 * d + c) * P
                        last = nc.tensor.transpose(M[2][:, (2 * i + c) * P:(2 * i + c + 1) * P], src[:, t:t + P],
                                                   ident[:])
                last.then_inc(sem("gdn_tr"), 1)

        def gdn_front_dve(dve, step, d):
            dve.wait_ge(sem("gdn_row"), d + 1)
            step(dve.tensor_tensor(wts[:].rearrange("p c (q t) -> p c q t", q=2),
                                   M[1][:].rearrange("p (c q t) -> p c q t", c=2, q=2),
                                   neg_mask[:].unsqueeze(1).broadcast_to([P, 2, 2, P]), ALU.add), "gdn_w")

        def gdn_front_act(act, step, d):
            act.wait_ge(sem("gdn_w"), d + 1)
            for c in range(2):
                t = 2 * d + c
                step(nc.scalar.activation(wts[:, c], wts[:, c], ACT.Exp, bias=gq[:, 2, t:t + 1]), "gdn_e" if c else None)

        def gdn_pe(pe, d, j):
            mm = nc.tensor.matmul
            if d < NT // 2 - 1 and j in (14, 15, 16):
                gdn_front_pe(pe, d + 1, j - 14)
            if j == 1:
                pe.wait_ge(sem("gdn_xt"), 7 * d + 1)
                for c in range(2):
                    last = nc.tensor.transpose(M[3][:, c * P:c * P + P], xmt[:, c], ident[:])
                last.then_inc(sem("gdn_x1"), 1)
            elif 2 <= j < 14:
                v = (j - 2) // 2
                b = LEVELS[v]
                if j % 2 == 0:
                    pe.wait_ge(sem("gdn_x"), 6 * d + v + 1)
                    pe.wait_ge(sem("gdn_xt"), 7 * d + v + 1)
                    for c in range(2):
                        last = mm(M[3][:, c * 64:c * 64 + 64], at[:, c, 0:P], one(xm[:, c], b, 0), start=True, stop=True)
                    last.then_inc(sem("gdn_p"), 1)
                else:
                    pe.wait_ge(sem("gdn_pm"), 6 * d + v + 1)
                    for c in range(2):
                        if v < len(LEVELS) - 1:
                            mm(M[3][:, 128 + c * 64:192 + c * 64], xmt[:, c], one(pm[:, v, c], b, 0), start=True,
                               stop=True)
                        last = mm(M[3][:, 256 + c * 64:320 + c * 64], pm[:, v, c], one(xmt[:, c], b, 1), start=True,
                                  stop=True)
                    last.then_inc(sem("gdn_q"), 1)
            elif j >= 14:
                c, s = divmod(j - 14, 3)
                t = 2 * d + c
                if s == 0:
                    pe.wait_ge(sem("gdn_s"), t + 1)
                    mm(M[4][:, 0:P], kq[:, 0, t * P:t * P + P], state_d[:], start=True, stop=True) \
                        .then_inc(sem("gdn_ks"), 1)
                elif s == 1:
                    pe.wait_ge(sem("gdn_r"), t + 1)
                    pe.wait_ge(sem("gdn_xt"), 7 * d + 7)
                    mm(M[4][:, P:2 * P], xmt[:, c], rhs[:], start=True, stop=True).then_inc(sem("gdn_vn"), 1)
                else:
                    if t:
                        pe.wait_ge(sem("gdn_y"), t)
                    pe.wait_ge(sem("gdn_qd"), d + 1)
                    mm(M[5][:, 0:P], qdec[:, c], state_d[:], start=True, stop=False)
                    pe.wait_ge(sem("gdn_vv"), t + 1)
                    mm(M[5][:, 0:P], at[:, c, P:2 * P], vnew[:], start=False, stop=True)
                    mm(M[4][:, 2 * P:3 * P], kend[:, c], vnew[:], start=True, stop=True).then_inc(sem("gdn_os"), 1)

        def gdn_act(act, step, d, j):
            A = nc.scalar.activation
            if d < NT // 2 - 1 and j == 17:
                gdn_front_act(act, step, d + 1)
            if j == 0:
                act.wait_ge(sem("gdn_tr"), d + 1)
                if d:
                    act.wait_ge(sem("gdn_os"), 2 * d)
                    act.wait_ge(sem("gdn_r"), 2 * d)
                for c in range(2):
                    t = 2 * d + c
                    step(A(kend[:, c], M[2][:, c * P:c * P + P], ACT.Copy, scale=gex[:, 1, t:t + 1]))
                    step(A(vbeta[:, c], M[2][:, (2 + c) * P:(3 + c) * P], ACT.Copy, scale=gh[:, 2, t:t + 1]),
                         "gdn_kv" if c else None)
            elif j == 1:
                act.wait_ge(sem("gdn_row"), d + 1)
                step(A(qdec[:], M[1][:].rearrange("p (c q t) -> p c q t", c=2, q=2)[:, :, 1], ACT.Exp), "gdn_eq")
            elif j >= 14:
                c, s = divmod(j - 14, 3)
                t = 2 * d + c
                if s == 1:
                    act.wait_ge(sem("gdn_vn"), t + 1)
                    step(A(vnew[:], M[4][:, P:2 * P], ACT.Copy), "gdn_vv")
                elif s == 2:
                    act.wait_ge(sem("gdn_os"), t + 1)
                    if t:
                        act.wait_ge(sem("gdn_y"), t)
                    step(A(junk[:, 0:P], M[5][:, 0:P], ACT.Square, accum_out=rs[:, 0:1]))
                    step(A(rs[:, 1:2], rs[:, 0:1], ACT.Ln, scale=1.0 / GDN_DV, bias=eps[:]))
                    step(A(rs[:, 2:3], rs[:, 1:2], ACT.Exp, scale=-0.5), "gdn_rms")

        def gdn_dve(dve, step, d, j):
            tt, stt = dve.tensor_tensor, dve.scalar_tensor_tensor
            if d < NT // 2 - 1 and j == 16:
                gdn_front_dve(dve, step, d + 1)
            if j == 0:
                if d == 0:
                    step(dve.memset(state_d[:], 0.0), "gdn_s")
                dve.wait_ge(sem("gdn_e"), d + 1)
                dve.wait_ge(sem("gdn_kq"), d + 1)
                step(tt(at[:].rearrange("p c n -> p (c n)"), M[0][:], wts[:].rearrange("p c n -> p (c n)"), ALU.mult),
                     "gdn_at")
                step(tt(xmt[:], at[:, :, 0:P], pair_mask[:].unsqueeze(1).broadcast_to([P, 2, P]), ALU.mult))
                step(tt(xmt[:], xmt[:], ident[:].unsqueeze(1).broadcast_to([P, 2, P]), ALU.add), "gdn_xt")
            elif j == 1:
                dve.wait_ge(sem("gdn_x1"), d + 1)
                step(dve.tensor_copy(xm[:].rearrange("p c n -> p (c n)"), M[3][:, 0:2 * P]), "gdn_x")
                dve.wait_ge(sem("gdn_eq"), d + 1)
                step(tt(qdec[:], qdec[:], kq[:, 1, 2 * d * P:2 * (d + 1) * P].rearrange("p (c t) -> p c t", c=2),
                        ALU.mult), "gdn_qd")
            elif 2 <= j < 14:
                v = (j - 2) // 2
                b = LEVELS[v]
                n = 64 // b

                def cols(o):
                    return M[3][:, o:o + 128].rearrange("p (c n b) -> p c n b", c=2, b=b)

                if j % 2 == 0:
                    dve.wait_ge(sem("gdn_p"), 6 * d + v + 1)
                    mask = level_mask[:, v].rearrange("p (n b) -> p n b", b=b).unsqueeze(1).broadcast_to([P, 2, n, b])
                    step(tt(pair(pm[:, v], b, 0), cols(0), mask, ALU.mult), "gdn_pm")
                else:
                    dve.wait_ge(sem("gdn_q"), 6 * d + v + 1)
                    if v < len(LEVELS) - 1:
                        step(tt(pair(xm[:], b, 0), pair(xm[:], b, 0), cols(128), ALU.subtract), "gdn_x")
                    step(tt(pair(xmt[:], b, 1), pair(xmt[:], b, 1), cols(256), ALU.subtract), "gdn_xt")
            elif j >= 14:
                c, s = divmod(j - 14, 3)
                t = 2 * d + c
                if s == 0:
                    dve.wait_ge(sem("gdn_ks"), t + 1)
                    dve.wait_ge(sem("gdn_kv"), d + 1)
                    step(stt(rhs[:], M[4][:, 0:P], gq[:, 3, t:t + 1], vbeta[:, c], ALU.mult, ALU.add), "gdn_r")
                elif s == 2:
                    dve.wait_ge(sem("gdn_os"), t + 1)
                    step(stt(state_d[:], state_d[:], gex[:, 2, t:t + 1], M[4][:, 2 * P:3 * P], ALU.mult, ALU.add),
                         "gdn_s")
                    dve.wait_ge(sem("gdn_rms"), t + 1)
                    if t >= 2:
                        dve.wait_ge(sem(f"y_out{t % 2}"), 16 * (t // 2))
                    step(stt(ybuf[:, t % 2, 0:P], M[5][:, 0:P], rs[:, 2:3], gdn_m[:, t], ALU.mult, ALU.mult), "gdn_y")

        def head_pe(pe):
            if br == "gla":
                pe.wait_ge(sem("g2_in"), 32)
                for half in range(2):
                    nc.tensor.matmul(M[half][:], w_g2[:], glr_t[:, half * HALF:half * HALF + HALF], start=True,
                                     stop=True).then_inc(sem("gla_g"), 1)

        def head_act(act, step):
            if br == "gla":
                for half in range(2):
                    s = slice(half * HALF, half * HALF + HALF)
                    act.wait_ge(sem("gla_g"), half + 1)
                    step(nc.scalar.activation(gabs[:], M[half][:], ACT.Abs, bias=b_g2[:]), "gla_abs")
                    step(nc.scalar.activation(gabs[:], gabs[:], ACT.Exp, scale=-1.0))
                    act.wait_ge(sem("gla_min"), half + 1)
                    step(nc.scalar.activation(gabs[:], gabs[:], ACT.Ln, bias=1.0), "gla_ln")
                    act.wait_ge(sem("gla_la"), half + 1)

        def head_dve(dve, step):
            step(dve.memset(state_g[:], 0.0), "g_s")
            if br == "gla":
                step(dve.memset(edge[:], 0.0))
                for half in range(2):
                    s = slice(half * HALF, half * HALF + HALF)
                    dve.wait_ge(sem("gla_abs"), half + 1)
                    step(dve.tensor_scalar(la[:, s], M[half][:], b_g2[:], 0.0, ALU.add, ALU.min), "gla_min")
                    dve.wait_ge(sem("gla_ln"), half + 1)
                    step(dve.tensor_tensor(la[:, s], la[:, s], gabs[:], ALU.subtract), "gla_la")
                step(dve.memset(M[0][:, 0:P], 0.0), "g_zero")
            else:
                mv = ml_g[:].rearrange("p q t h -> p (q t) h")
                step(dve.tensor_copy(mh[:].rearrange("p q t -> p (q t)").unsqueeze(2), mv[:, :, ds(f, 1)]), "ml_mh")

        def prep_act(act, step, c, stage):
            A = nc.scalar.activation
            if stage == 0:
                act.wait_ge(sem("gla_cum"), c + 1)
                if c:
                    act.wait_ge(sem("g_sc"), c)
                if c >= 2:
                    act.wait_ge(sem("g_os"), c - 1)
                step(A(dq[:], dq[:], ACT.Exp, scale=1.0 / GLA_GATE_NORM, bias=ln_dk[:]))
                step(A(qd[:, c % 2], cum[:], ACT.Exp, scale=1.0 / GLA_GATE_NORM, bias=ln_dk[:]))
                step(A(dl_col[:, c:c + 1], last16[:], ACT.Exp), "gla_dl")
                step(A(ke[:], cum[:], ACT.Exp, scale=-1.0 / GLA_GATE_NORM, bias=last16[:]), "gla_ee")
            for i in range(4 * stage, 4 * stage + 4):
                n = SUB * (i + 1)
                step(A(kt_sub[:, i, 0:n], cum[:, 0:n], ACT.Exp, scale=-1.0 / GLA_GATE_NORM,
                       bias=edge[:, 1, i:i + 1]), "gla_ek" if i % 4 == 3 else None)

        def prep_dve(dve, step, c):
            cs = slice(c * P, c * P + P)
            if c:
                dve.wait_ge(sem("gla_ek"), 2 * c)
            step(dve.tensor_tensor_scan(cum[:], ones[:], la[:, cs], 0.0, ALU.mult, ALU.add))
            step(dve.tensor_copy(edge[:, 0, 1:NT], cum[:, SUB - 1:P - 1:SUB]))
            step(dve.tensor_scalar(edge[:, 1], edge[:, 0], 1.0 / GLA_GATE_NORM, None, ALU.mult))
            step(dve.tensor_scalar(last16[:], cum[:, P - 1:P], 1.0 / GLA_GATE_NORM, None, ALU.mult))
            if c:
                dve.wait_ge(sem("g_sc"), c)
            step(dve.tensor_tensor(dq[:].rearrange("p (n s) -> p n s", s=SUB),
                                   cum[:].rearrange("p (n s) -> p n s", s=SUB),
                                   edge[:, 0].unsqueeze(2).broadcast_to([P, NT, SUB]), ALU.subtract), "gla_cum")

        def prep_pool(pool, step, c):
            cs = slice(c * P, c * P + P)
            if c == 0:
                pool.wait_ge(sem("proj_read1"), 2)
                pool.wait_ge(sem("proj_read0"), 2)
            pool.wait_ge(sem("gla_ee"), c + 1)
            step(pool.tensor_tensor(dq[:], qg[:, cs], dq[:], ALU.mult))
            step(pool.tensor_tensor(qd[:, c % 2], qg[:, cs], qd[:, c % 2], ALU.mult))
            step(pool.tensor_tensor(ke[:], kg[:, cs], ke[:], ALU.mult))
            for half in range(2):
                n = 64 * (half + 1)
                sub = kt_sub[:, 4 * half:4 * half + 4, 0:n]
                pool.wait_ge(sem("gla_ek"), 2 * c + half + 1)
                step(pool.tensor_tensor(sub, sub, kg[:, c * P:c * P + n].unsqueeze(1).broadcast_to([P, 4, n]), ALU.mult),
                     "gla_prep" if half else None)

        def chunk_pe(pe, c, stage):
            mm = nc.tensor.matmul
            cs = slice(c * P, c * P + P)
            n = GLA_DV if br == "gla" else GLA_DV + 1
            if stage == 0:
                if c:
                    pe.wait_ge(sem("g_scd"), c)
                    pe.wait_ge(sem("g_kend"), c)
                if br == "gla":
                    pe.wait_ge(sem("gla_prep"), c + 1)
                    if c == 0:
                        pe.wait_ge(sem("g_zero"), 1)
                    for i in range(P // SUB):
                        n_s = SUB * (i + 1)
                        mm(M[0][0:n_s, i * SUB:n_s], kt_sub[:, i, 0:n_s], dq[:, i * SUB:n_s], start=True, stop=True)
                    nc.tensor.transpose(M[2][:, 0:P], ke[:], ident[:]).then_inc(sem("g_sc"), 1)
                else:
                    if c == 0:
                        pe.wait_ge(sem("ml_mh"), 1)
                    if c:
                        pe.wait_ge(sem("ml_eq"), c)
                    mm(M[0][:, 0:P], kg[:, cs], qg[:, cs], start=True, stop=True)
                    mm(M[1][:, 0:P], mh[:, 0, c:c + 1].broadcast_to([P, P]), ident[:], start=True, stop=True)
                    nc.tensor.transpose(M[2][:, 0:P], kg[:, cs], ident[:]).then_inc(sem("g_sc"), 1)
            else:
                pe.wait_ge(sem("g_scd"), c + 1)
                pe.wait_ge(sem("g_s"), c + 1)
                if c:
                    pe.wait_ge(sem("g_y"), c)
                if br == "ml":
                    pe.wait_ge(sem("ml_qd"), c + 1)
                mm(M[3][:, 0:n], sc[:], vg[:, c, 0:n], start=True, stop=False)
                mm(M[3][:, 0:n], qd[:, c % 2], state_g[:, 0:n], start=False, stop=True)
                pe.wait_ge(sem("g_kend"), c + 1)
                mm(M[4][:, 0:n], kend_g[:], vg[:, c, 0:n], start=True, stop=True).then_inc(sem("g_os"), 1)

        def chunk_act(act, step, c, stage):
            A = nc.scalar.activation
            if stage == 0:
                act.wait_ge(sem("g_sc"), c + 1)
                if c:
                    act.wait_ge(sem("g_os"), c)
                if br == "gla":
                    step(A(kend_g[:], M[2][:, 0:P], ACT.Copy), "g_kend")
                else:
                    step(A(kend_g[:], M[2][:, 0:P], ACT.Copy, scale=mh[:, 3, c:c + 1]), "g_kend")
                    act.wait_ge(sem("ml_w"), c + 1)
                    step(A(dq[:], dq[:], ACT.Exp, bias=mh[:, 1, c:c + 1]), "ml_e")
                    step(A(qd[:, c % 2], M[1][:, 0:P], ACT.Exp, bias=mh[:, 2, c:c + 1]), "ml_eq")
            else:
                act.wait_ge(sem("g_os"), c + 1)
                if c:
                    act.wait_ge(sem("g_y"), c)
                step(A(junk[:], M[3][:, 0:GLA_DV], ACT.Square, accum_out=rs[:, 0:1]))
                if br == "gla":
                    step(A(rs[:, 1:2], rs[:, 0:1], ACT.Ln, scale=1.0 / GLA_DV, bias=eps[:]))
                    step(A(rs[:, 2:3], rs[:, 1:2], ACT.Exp, scale=-0.5), "g_rms")
                else:
                    step(A(rs[:, 1:2], M[3][:, GLA_DV:GLA_DV + 1], ACT.Abs), "ml_den")
                    act.wait_ge(sem("ml_ms"), c + 1)
                    step(A(rs[:, 2:3], rs[:, 2:3], ACT.Ln, scale=1.0 / GLA_DV, bias=eps[:]))
                    step(A(rs[:, 2:3], rs[:, 2:3], ACT.Exp, scale=-0.5), "g_rms")

        def chunk_dve(dve, step, c, stage):
            tt, stt = dve.tensor_tensor, dve.scalar_tensor_tensor
            n = GLA_DV if br == "gla" else GLA_DV + 1
            if stage == 0:
                dve.wait_ge(sem("g_sc"), c + 1)
                if br == "gla":
                    if c:
                        dve.wait_ge(sem("g_os"), c)
                    step(tt(sc[:], M[0][:, 0:P], tri[:], ALU.mult), "g_scd")
                else:
                    step(tt(dq[:], M[1][:, 0:P], neg_mask[:, 1], ALU.add), "ml_w")
                    dve.wait_ge(sem("ml_e"), c + 1)
                    step(tt(sc[:], M[0][:, 0:P], dq[:], ALU.mult), "g_scd")
                    dve.wait_ge(sem("ml_eq"), c + 1)
                    step(tt(qd[:, c % 2], qg[:, c * P:c * P + P], qd[:, c % 2], ALU.mult), "ml_qd")
            else:
                dve.wait_ge(sem("g_os"), c + 1)
                if br == "gla":
                    dve.wait_ge(sem("gla_dl"), c + 1)
                decay = dl_col[:, c:c + 1] if br == "gla" else mh[:, 4, c:c + 1]
                step(stt(state_g[:, 0:n], state_g[:, 0:n], decay, M[4][:, 0:n], ALU.mult, ALU.add), "g_s")
                if br == "ml":
                    dve.wait_ge(sem("ml_den"), c + 1)
                    step(tt(rs[:, 1:2], rs[:, 1:2], mh[:, 5, c:c + 1], ALU.max))
                    step(dve.reciprocal(rs[:, 3:4], rs[:, 1:2]))
                    step(tt(rs[:, 2:3], rs[:, 3:4], rs[:, 3:4], ALU.mult))
                    step(tt(rs[:, 2:3], rs[:, 2:3], rs[:, 0:1], ALU.mult), "ml_ms")
                dve.wait_ge(sem("g_rms"), c + 1)
                if br == "ml":
                    step(tt(rs[:, 2:3], rs[:, 2:3], rs[:, 3:4], ALU.mult))
                dve.wait_ge(sem(f"y_out{c % 2}"), 16 * ((NT + c) // 2))
                step(stt(ybuf[:, c % 2], M[3][:, 0:GLA_DV], rs[:, 2:3], mg[:, c], ALU.mult, ALU.mult), "g_y")

        CONV_AT = (7, 20, 33)

        def conv_dve(dve, step, b):
            for j in range(3):
                o = b - CONV_AT[j]
                e = conv_in[:, j % 2, GDN_TAPS - 1:]
                if o in range(GDN_TAPS):
                    src = conv_in[:, j % 2, o:o + S]
                    w = conv_w[:, o, j:j + 1]
                    if o == 0:
                        if j:
                            dve.wait_ge(sem("conv_silu"), j)
                        for u in (u0 + (0, 2, 8)[j], u0 + (1, 3, 9)[j]):
                            dve.wait_ge(sem(f"proj_read{u % 2}"), u // 2 + 1)
                        step(dve.tensor_scalar(conv_acc[:], src, w, None, ALU.mult))
                    else:
                        step(dve.scalar_tensor_tensor(conv_acc[:], src, w, conv_acc[:], ALU.mult, ALU.add),
                             "conv" if o == GDN_TAPS - 1 else None)
                elif o == 8:
                    dve.wait_ge(sem("conv_e"), j + 1)
                    step(dve.scalar_tensor_tensor(e, conv_acc[:], 0.0, e, ALU.min, ALU.subtract), "conv_ls")
                elif o == 10 and j == 2:
                    dve.wait_ge(sem("conv_sig"), j + 1)
                    step(dve.tensor_tensor(v_t[:], conv_acc[:], e, ALU.mult))

        def conv_pool(pool, step, b):
            for j in range(2):
                if b == CONV_AT[j] + 10:
                    pool.wait_ge(sem("conv_sig"), j + 1)
                    step(pool.tensor_tensor((kq[:, 1], kq[:, 0])[j], conv_acc[:], conv_in[:, j, GDN_TAPS - 1:], ALU.mult),
                         "conv_silu")

        def conv_act(act, step, b):
            A = nc.scalar.activation
            for j in range(3):
                o = b - CONV_AT[j]
                e = conv_in[:, j % 2, GDN_TAPS - 1:]
                if o == 4:
                    act.wait_ge(sem("conv"), j + 1)
                    step(A(e, conv_acc[:], ACT.Abs))
                elif o == 5:
                    step(A(e, e, ACT.Exp, scale=-1.0))
                elif o == 6:
                    step(A(e, e, ACT.Ln, bias=1.0), "conv_e")
                elif o == 9:
                    act.wait_ge(sem("conv_ls"), j + 1)
                    step(A(e, e, ACT.Exp), "conv_sig")
                elif o == 12 and j < 2:
                    act.wait_ge(sem("conv_silu"), j + 1)
                    step(A(e, (kq[:, 1], kq[:, 0])[j], ACT.Square), "conv_sq")

        def conv_pe(pe, b):
            for j in range(2):
                if b == CONV_AT[j] + 15:
                    pe.wait_ge(sem("conv_sq"), j + 1)
                    for t in range(NT):
                        o = GDN_TAPS - 1 + t * P
                        mm = nc.tensor.matmul(M[5][:, j * NT + t:j * NT + t + 1], conv_in[:, j % 2, o:o + P], ones[:, 0:1],
                                              start=True, stop=True)
                    mm.then_inc(sem("conv_ss"), 1)

        def gates_act(act, step, b):
            if b == 36:
                act.wait_ge(sem("conv_ss"), 2)
                step(nc.scalar.activation(lnss[:].rearrange("p q t -> p (q t)"), M[5][:, 0:2 * NT], ACT.Ln,
                                          bias=eps[:]), "gate_ln")
            if b == 38:
                act.wait_ge(sem("gate_pre"), 1)
                step(nc.scalar.activation(gex[:], gex[:], ACT.Exp), "gate_e")

        def gates_dve(dve, step, b):
            tt, stt = dve.tensor_tensor, dve.scalar_tensor_tensor
            if b == 6:
                wv = conv_col[:].rearrange("p (j i h) -> p (j i) h", i=3, h=GDN_H)
                step(dve.tensor_copy(conv_w[:].rearrange("p j i -> p (j i)").unsqueeze(2), wv[:, :, ds(next_h, 1)]))
            if b == 37:
                gv = gdn_g[:].rearrange("p q t h -> p (q t) h")
                step(dve.tensor_copy(gh[:].rearrange("p q t -> p (q t)").unsqueeze(2), gv[:, :, ds(next_h, 1)]))
                dve.wait_ge(sem("gate_ln"), 1)
                step(stt(gq[:, 2], lnss[:, 1], -0.5, gh[:, 0], ALU.mult, ALU.subtract))
                step(stt(gq[:, 1], lnss[:, 0], -0.5, gh[:, 0], ALU.mult, ALU.add))
                step(dve.tensor_scalar(gq[:, 1], gq[:, 1], LN_DK, None, ALU.add))
                step(stt(gex[:, 0], lnss[:, 1], -0.5, gh[:, 0], ALU.mult, ALU.add))
                step(tt(gq[:, 0], gex[:, 0], gh[:, 1], ALU.add))
                step(tt(gex[:, 1], gh[:, 3], gq[:, 2], ALU.add))
                step(dve.tensor_copy(gex[:, 2], gh[:, 3]), "gate_pre")
            if b == 39:
                dve.wait_ge(sem("gate_e"), 1)
                step(stt(gq[:, 3], gex[:, 0], -1.0, gh[:, 2], ALU.mult, ALU.mult))

        n1 = 4 * BEATS1 if br else 0
        n2 = 50
        scores = [n1 + PRE2 + CHUNK2 * c for c in range(5, NT)] if br == "gla" else []
        pieces = [2 if b < n1 and b % BEATS1 == 1 else 0 if b in scores else 1 for b in range(n1 + n2)]
        piece_at = [sum(pieces[:b]) for b in range(n1 + n2 + 1)]
        unit_done = {u: min(b for b in range(n1 + n2) if piece_at[b + 1] >= 3 * u + 3) for u in range(n_units)}
        if br:
            after = {g: unit_done[u] + 1 for g, u in last_unit.items()}
            LOAD_AT = {1: 0, 2: 8, 3: 20, 4: 44, 5: 64, 6: n1 + 1, 7: n1 + 10}
            SPLIT_AT = {1: (0, 0), 2: (after[0], after[0]), 3: (after[1], after[1]), 4: (after[2], after[2]),
                        5: (after[3], after[3]), 6: (n1 + 9, n1 + 9), 7: (n1 + 14, n1 + 19)}
        else:
            LOAD_AT = {1: 0, 2: 1, 3: 2}
            SPLIT_AT = {1: (0, 0), 2: (1, 1), 3: (13, 13)}

        with nc.Block() as block:
            @block.sync
            def _(sp):
                if br == "gla":
                    sp.dma_start(w_g2[:], gla_w_g2[:, ds(f * P, P)]).then_inc(sem("g2_in"), 16)
                    sp.dma_start(b_g2[:], gla_b_g2.rearrange("(n a) -> n a", a=1)[ds(f * P, P), :]) \
                        .then_inc(sem("g2_in"), 16)
                for b in range(n1 + n2 + 1):
                    for n in range(EARLY if last else 0):
                        if b == (n1 + max(EARLY_AT[n] - 12, 1) if n else 50):
                            if n == 0:
                                sp.wait_ge(sem("w_split"), 12)
                            if n == 1:
                                sp.wait_ge(sem("gdn_y"), NT)
                            gather_sp(sp, n, n, early_parts)
                    if last and b - n1 in W_EARLY_AT:
                        m = W_EARLY_AT.index(b - n1)
                        if m == 0:
                            sp.wait_ge(sem("sig_used"), 2 * NT)
                            for j in range(2):
                                sp.dma_start(gain_g[:, j], gates_dram[0, j * 256:(j + 1) * 256].partition_broadcast(P)) \
                                    .then_inc(sem("gates_in"), 16)
                        else:
                            sp.wait_ge(sem("out_split"), m)
                        sp.dma_start(w_raw[:, 1], out_v[:, :, m * P:m * P + P]).then_inc(sem("out_in"), 16)
                    for g in range(1, len(groups)):
                        if LOAD_AT[g] == b:
                            for i in range(2):
                                if g >= 2:
                                    sp.wait_ge(sem("w_split"), 4 * (g - 2) + 2 * (i + 1))
                                load_half(sp, i, groups[g][1][i])
                    if not br:
                        continue
                    for t in range(NT):
                        if b == BEATS1 * (t // 2) + 17 + 3 * (t % 2):
                            sp.wait_ge(sem("gdn_y"), t + 1)
                            sp.dma_start(y_dram[2, t * P:t * P + P, ds(h * P, P)], ybuf[:, t % 2, 0:P]) \
                                .then_inc(sem(f"y_out{t % 2}"), 16)
                        if b == n1 + PRE2 + CHUNK2 * t + 4:
                            sp.wait_ge(sem("g_y"), t + 1)
                            sp.dma_start(y_dram[0 if br == "gla" else 1, t * P:t * P + P, ds(f * GLA_DV, GLA_DV)],
                                         ybuf[:, t % 2]).then_inc(sem(f"y_out{t % 2}"), 16)
                if br:
                    for i in range(2):
                        sp.wait_ge(sem(f"y_out{i}"), 16 * NT)

            @block.gpsimd
            def _(pool):
                own = Count(sem("w_split"))
                step = Steps(pool, "pool_step")
                for b in range(n1 + n2):
                    c, s = divmod(b - n1 - 3, CHUNK2)
                    if br == "gla" and s == 0 and 0 <= c < NT:
                        prep_pool(pool, step, c)
                    if last and b - n1 in W_EARLY_AT:
                        m = W_EARLY_AT.index(b - n1)
                        if m == 0:
                            pool.wait_ge(sem("proj0"), U1 // 2)
                            pool.wait_ge(sem("proj1"), U1 // 2)
                            pool.wait_ge(sem("gates_in"), 32)
                        pool.wait_ge(sem("out_in"), 16 * (m + 1))
                        gate = gain_g[:, m // 2, m % 2 * P:(m % 2 + 1) * P].unsqueeze(1).broadcast_to([P, KT, P])
                        hi, lo = (w[:, :, m % 2 * P:(m % 2 + 1) * P] for w in (A_W, B_W)[m // 2])
                        step(pool.tensor_tensor(w_raw[:, 1], w_raw[:, 1], gate, ALU.mult))
                        step(pool.tensor_copy(hi, w_raw[:, 1]))
                        step(pool.tensor_tensor(lo, w_raw[:, 1], hi.bitcast(F32), ALU.subtract), "out_split")
                    if next_h is not None:
                        conv_pool(pool, step, b - n1)
                    for u in range(u0, n_units):
                        if unit_done[u] + 3 == b:
                            pool_unit(pool, u)
                    for g in range(1, len(groups)):
                        buf, _, width = groups[g]
                        for i in range(2):
                            if SPLIT_AT[g][i] != b:
                                continue
                            before = [k for k in range(g) if groups[k][0] == buf]
                            if before and i == 0:
                                u = last_unit[before[-1]]
                                pool.wait_ge(sem(f"proj{u % 2}"), u // 2 + 1)
                            pool.wait_ge(sem(f"w_in{i}"), 16 * g)
                            split(pool, i, w_buf[buf], width // 2, own)

            @block.tensor
            def _(pe):
                if br:
                    for part in range(3):
                        gdn_front_pe(pe, 0, part)
                for b in range(n1 + n2):
                    start, end = piece_at[b], min(piece_at[b + 1], 3 * n_units)
                    if b < n1:
                        if b % BEATS1 == 1:
                            piece(pe, start)
                            start += 1
                        gdn_pe(pe, b // BEATS1, b % BEATS1)
                    elif br:
                        if b == n1:
                            head_pe(pe)
                        c, s = divmod(b - n1 - PRE2, CHUNK2)
                        if 0 <= c < NT and s in (0, 3):
                            chunk_pe(pe, c, s // 3)
                    if next_h is not None:
                        conv_pe(pe, b - n1)
                    elif b - n1 in EARLY_AT:
                        gather_pe(pe, EARLY_AT.index(b - n1), early_parts)
                    for n in range(start, end):
                        piece(pe, n)

            @block.scalar
            def _(act):
                step = Steps(act, "act_step")
                nc.scalar.preload_act_table_set("natural_log_exp_and_others")
                if br:
                    gdn_front_act(act, step, 0)

                def act_units(b):
                    for u in range(n_units):
                        if unit_done[u] + 1 == b:
                            act_unit(act, step, u)

                for b in range(n1 + n2):
                    if b >= n1:
                        act_units(b)
                    if b < n1:
                        gdn_act(act, step, b // BEATS1, b % BEATS1)
                    elif br:
                        if b == n1:
                            head_act(act, step)
                        c, s = divmod(b - n1 - PRE2, CHUNK2)
                        if 0 <= c < NT and s in (0, 3):
                            chunk_act(act, step, c, s // 3)
                        c, s = divmod(b - n1 - 2, CHUNK2)
                        if br == "gla" and s < 2 and 0 <= c < NT:
                            prep_act(act, step, c, s)
                    if next_h is not None:
                        conv_act(act, step, b - n1)
                        gates_act(act, step, b - n1)
                    elif b - n1 in EARLY_AT:
                        n = EARLY_AT.index(b - n1)
                        if n == 0:
                            act.wait_ge(sem("proj0"), U1 // 2)
                            act.wait_ge(sem("proj1"), U1 // 2)
                        gather_hi(act, n, n)
                    if b < n1:
                        act_units(b)

            @block.vector
            def _(dve):
                step = Steps(dve, "dve_step")
                if br:
                    gdn_front_dve(dve, step, 0)
                for b in range(n1 + n2):
                    if b < n1:
                        gdn_dve(dve, step, b // BEATS1, b % BEATS1)
                    elif br:
                        if b == n1:
                            head_dve(dve, step)
                        c, s = divmod(b - n1 - PRE2, CHUNK2)
                        if 0 <= c < NT and s in (0, 3):
                            chunk_dve(dve, step, c, s // 3)
                        c, s = divmod(b - n1 - 1, CHUNK2)
                        if br == "gla" and s == 0 and 0 <= c < NT:
                            prep_dve(dve, step, c)
                    if next_h is not None:
                        gates_dve(dve, step, b - n1)
                        conv_dve(dve, step, b - n1)
                    else:
                        for n, at_ in enumerate(EARLY_AT):
                            if b == n1 + at_ - 1:
                                gather_sum(dve, n, early_parts)
                            if b == n1 + at_ + 2:
                                gather_lo(dve, n, n)
                    for u in range(n_units):
                        for stage in range(3):
                            if unit_done[u] + 1 + stage == b:
                                dve_unit(dve, step, u, stage)
        end_section()

    with nc.Block() as block:
        @block.sync
        def _(sp):
            for i, v in enumerate((gla_norm, ml_norm)):
                sp.dma_start(gain_g[:, i], v.partition_broadcast(P)).then_inc(sem("gain_in"), 16)
            sp.dma_start(gain_d[:], gdn_norm.partition_broadcast(P)).then_inc(sem("gain_in"), 16)
            sp.wait_ge(sem("gain_in"), 48)

        @block.vector
        def _(dve):
            own = Count(sem("cleared"))
            own.inc(dve.memset(conv_in[:, :, 0:GDN_TAPS - 1], 0.0))
            own.inc(dve.memset(pm[:], 0.0))
            own.inc(dve.memset(kt_sub[:], 0.0))
            own.inc(dve.memset(vg[:], 1.0))
            own.wait(dve)
    end_section()
    mixer_section(None, None, None, 0, gla_cols("gla", 0)[0])
    with nc.Fori(0, GLA_H) as f:
        last = (f + 1) >> 2
        q, k = ((f + 1) * P + (last * (COL["ml_" + n] - COL["gla_" + n] - GLA_H * P) + COL["gla_" + n]) for n in "qk")
        mixer_section("gla", f, f, f + 1, qk_cols(q, k))
    with nc.Fori(0, ML_H - 1) as f:
        mixer_section("ml", f, f + GLA_H, f + (GLA_H + 1), gla_cols("ml", f + 1)[0])
    mixer_section("ml", ML_H - 1, GDN_H - 1, None, None)
    mixers.close()
    inproj.close()

    x1 = sb("x1", [P, NT, D])
    gates = sb("gates", [P, 2, D])
    out_proj = ExitStack()
    O_W = [A_W, B_W] + [[sb(f"w{n}_{h}", [P, KT, 256], F32R, stack=out_proj) for h in ("hi", "lo")] for n in "EF"]
    y_parts = sb("y_parts", [P, 2, 3, S], stack=out_proj)
    late_parts = [[by_tile(y_parts[:, n, b]) for b in range(3)] for n in range(2)]
    normed, sq = y_parts[:, 0, 0:2], y_parts[:, 0, 2]
    full = y_parts[:, 1, 0].rearrange("p (q k n) -> p q k n", q=2, n=P)
    ss = sb("ss", [P, NT], stack=out_proj)
    rstd = sb("rstd", [P, NT], stack=out_proj)
    up_v = w_ffn_up.rearrange("(k p) n -> p k n", p=P)
    down_v = w_ffn_down.rearrange("(k p) n -> p k n", p=P)
    F_STEPS = D_FF // (2 * P)
    N_OUT = 2 * (D // 256)

    def up_cols(n):
        return [up_v[:, :, ds(n * P, P)], up_v[:, :, ds(n * P + D_FF, P)]]

    order = [(t, 0) for t in range(NT)] + [(t, g) for t in range(NT) for g in range(1, 4)]
    OUT_BANKS, UP_BANKS = banks[0:6], banks[6:8]

    def tile_done(t):
        return NT + 3 * (t + 1)

    with nc.Block() as block:
        @block.sync
        def _(sp):
            for i in range(2):
                sp.dma_start(gates[:, i], gates_dram[i].partition_broadcast(P)).then_inc(sem("gates_in"), 16)
            for n in range(KT - EARLY):
                gather_sp(sp, n, EARLY + n, late_parts)
            for m in range(W_EARLY, N_OUT):
                i = m % 2
                if m >= W_EARLY + 2:
                    sp.wait_ge(sem("out_split"), m - W_EARLY - 1)
                sp.dma_start(w_raw[:, i], out_v[:, :, m * P:m * P + P]).then_inc(sem(f"w_in{i}"), 16)
                if m == W_EARLY + 1:
                    sp.dma_start(x1[:], x.rearrange("(t p) d -> p t d", p=P)).then_inc(sem("x_in"), 16)
            for i in range(2):
                sp.wait_ge(sem("out_split"), N_OUT - W_EARLY - 1 + i)
                load_half(sp, i, up_cols(0)[i])

        @block.gpsimd
        def _(pool):
            own = Count(sem("w_split"))
            for g in range(2):
                pool.wait_ge(sem("proj"), NT)
                pool.wait_ge(sem(f"w_in{g}"), 16 * ((N_OUT - W_EARLY) // 2 + 1))
                split(pool, g, A_W, P, own)

        @block.tensor
        def _(pe):
            for n in range(KT - EARLY):
                gather_pe(pe, n, late_parts)
            pe.wait_ge(sem("gather_lo"), 2 * (KT - EARLY))

            def norm_up(t):
                for q in range(2):
                    pe.wait_ge(sem("normed"), t + 1)
                    if t:
                        pe.wait_ge(sem("scaled"), 2 * t - 1 + q)
                    for j in range(4):
                        tp = nc.tensor.transpose(UP_BANKS[q][:, j * P:j * P + P],
                                                 normed[:, t % 2, (4 * q + j) * P:(4 * q + j + 1) * P], ident[:])
                    tp.then_inc(sem("norm_up"), 1)

            for n, (t, g) in enumerate(order):
                if g >= W_EARLY // 2:
                    pe.wait_ge(sem("out_split"), 2 * g + 2 - W_EARLY)
                if n >= 6:
                    pe.wait_ge(sem("out_read"), n - 5)
                token_major(OUT_BANKS[n % 6], t, O_W[g], 0, 256, range(3 * KT)).then_inc(sem("proj"), 1)
                if g == 3 and t:
                    norm_up(t - 1)
            norm_up(NT - 1)

        @block.scalar
        def _(act):
            nc.scalar.preload_act_table_set("natural_log_exp_and_others")
            own = Count(sem("rms"))
            for m in range(2):
                gather_hi(act, m, EARLY + m)
            for m in range(W_EARLY, N_OUT):
                act.wait_ge(sem("out_gated"), m + 1 - W_EARLY)
                i = m % 2
                nc.scalar.activation(O_W[m // 2][0][:, :, i * P:i * P + P], w_raw[:, i], ACT.Copy) \
                    .then_inc(sem("out_hi"), 1)
            for t in range(NT):
                act.wait_ge(sem("out_read"), tile_done(t))
                own.inc(nc.scalar.activation(sq, x1[:, t], ACT.Square, accum_out=ss[:, t:t + 1]))
                own.wait(act)
                own.inc(nc.scalar.activation(ss[:, t:t + 1], ss[:, t:t + 1], ACT.Ln, scale=1.0 / D, bias=eps[:]))
                own.wait(act)
                nc.scalar.activation(rstd[:, t:t + 1], ss[:, t:t + 1], ACT.Exp, scale=-0.5).then_inc(sem("rstd"), 1)
                for q in range(2):
                    act.wait_ge(sem("full"), 2 * t + q + 1)
                    nc.scalar.activation(h_hi[:, 4 * q:4 * q + 4, t * P:t * P + P], full[:, q], ACT.Copy) \
                        .then_inc(sem("norm_hi"), 1)

        @block.vector
        def _(dve):
            for m in range(KT - EARLY):
                gather_sum(dve, m, late_parts)
                gather_lo(dve, m, EARLY + m)
            dve.wait_ge(sem("gates_in"), 32)
            for m in range(W_EARLY, N_OUT):
                i = m % 2
                dve.wait_ge(sem(f"w_in{i}"), 16 * ((m - W_EARLY) // 2 + 1))
                gate = gates[:, 0, m * P:m * P + P].unsqueeze(1).broadcast_to([P, KT, P])
                dve.tensor_tensor(w_raw[:, i], w_raw[:, i], gate, ALU.mult).then_inc(sem("out_gated"), 1)
                dve.wait_ge(sem("out_hi"), m + 1 - W_EARLY)
                hi, lo = (w[:, :, i * P:i * P + P] for w in O_W[m // 2])
                dve.tensor_tensor(lo, w_raw[:, i], hi.bitcast(F32), ALU.subtract).then_inc(sem("out_split"), 1)
            dve.wait_ge(sem("x_in"), 16)

            def norm_scale(t):
                dve.wait_ge(sem("rstd"), t + 1)
                if t >= 2:
                    dve.wait_ge(sem("norm_up"), 2 * t - 2)
                dve.tensor_scalar(normed[:, t % 2], x1[:, t], rstd[:, t:t + 1], None, ALU.mult) \
                    .then_inc(sem("normed"), 1)

            def norm_split(t):
                for q in range(2):
                    scale, shift = (mod_col[:, i, 4 * q:4 * q + 4].unsqueeze(2).broadcast_to([P, 4, P]) for i in (2, 3))
                    dve.wait_ge(sem("norm_up"), 2 * t + q + 1)
                    if t:
                        dve.wait_ge(sem("norm_lo"), 2 * t - 1 + q)
                    dve.tensor_tensor(full[:, q], UP_BANKS[q][:].rearrange("p (k n) -> p k n", n=P), scale, ALU.mult) \
                        .then_inc(sem("scaled"), 1)
                    dve.wait_ge(sem("scaled"), 2 * t + q + 1)
                    dve.tensor_tensor(full[:, q], full[:, q], shift, ALU.add).then_inc(sem("full"), 1)
                for q in range(2):
                    dve.wait_ge(sem("norm_hi"), 2 * t + q + 1)
                    dve.tensor_tensor(h_lo[:, 4 * q:4 * q + 4, t * P:t * P + P], full[:, q],
                                      h_hi[:, 4 * q:4 * q + 4, t * P:t * P + P].bitcast(F32), ALU.subtract) \
                        .then_inc(sem("norm_lo"), 1)

            for n, (t, g) in enumerate(order):
                cols = slice(g * 256, g * 256 + 256)
                dve.wait_ge(sem("proj"), n + 1)
                dve.tensor_tensor(x1[:, t, cols], x1[:, t, cols], OUT_BANKS[n % 6][:, 0:256], ALU.add) \
                    .then_inc(sem("out_read"), 1)
                if g == 1 and t >= 2:
                    norm_split(t - 2)
                if g == 2 and t:
                    norm_scale(t - 1)
            dve.wait_ge(sem("out_read"), len(order))
            norm_split(NT - 2)
            norm_scale(NT - 1)
            norm_split(NT - 1)
    end_section()
    out_proj.close()

    D_W = [sb(f"wD_{h}", [P, 2, D], F32R) for h in ("hi", "lo")]
    hid = [sb(f"hid_{h}", [P, 2, S], F32R) for h in ("hi", "lo")]
    e_buf = sb("e_buf", [P, 2, HALF])
    fin_gain = sb("fin_gain", [P, D])

    f_ss = sb("f_ss", [P, NT])
    f_junk = sb("f_junk", [P, D])
    f_rstd = sb("f_rstd", [P, NT])

    def ffn_pass(i, last):
        UP, DOWN = banks[0:4], banks[4:8]
        n_groups = 2 if last else 3

        with nc.Block() as block:
            @block.sync
            def _(sp):
                for j, src in enumerate(up_cols(2 * i + 1)):
                    load_half(sp, j, src)
                for j in range(2):
                    sp.wait_ge(sem("w_split"), 2 * j + 2)
                    sp.dma_start(w_raw[:, j].rearrange("p k n -> p (k n)"), down_v[:, ds(2 * i + j, 1)].squeeze(1)).then_inc(sem(f"w_in{j}"), 16)
                if not last:
                    for j, src in enumerate(up_cols(2 * i + 2)):
                        sp.wait_ge(sem("w_split"), 4 + 2 * j + 2)
                        load_half(sp, j, src)
                else:
                    sp.dma_start(fin_gain[:], norm_final.partition_broadcast(P)).then_inc(sem("gain_in"), 16)
                    for t in range(NT):
                        sp.wait_ge(sem("out_ready"), t + 1)
                        sp.dma_start(out[t * P:t * P + P, :], x1[:, t]).then_inc(sem("out_stored"), 16)
                    sp.wait_ge(sem("out_stored"), 16 * NT)

            @block.gpsimd
            def _(pool):
                own, gated = Count(sem("w_split")), Count(sem("w_gated"))
                for g in range(n_groups):
                    if g == 2:
                        pool.wait_ge(sem("up"), 4)
                    for j in range(2):
                        pool.wait_ge(sem(f"w_in{j}"), 16 * (g + 1))
                        if g == 1:
                            raw = w_raw[:, j].rearrange("p k n -> p (k n)")
                            gated.inc(pool.tensor_tensor(raw, raw, gates[:, 1], ALU.mult))
                            gated.wait(pool)
                            own.inc(pool.tensor_copy(D_W[0][:, j], raw))
                            own.wait(pool)
                            own.inc(pool.tensor_tensor(D_W[1][:, j], raw, D_W[0][:, j].bitcast(F32), ALU.subtract))
                            own.wait(pool)
                        else:
                            split(pool, j, (B_W, None, A_W)[g], P, own)

            @block.tensor
            def _(pe):
                for u in range(8):
                    k, half, gv = u // 4, u // 2 % 2, u % 2
                    if u == 4:
                        pe.wait_ge(sem("w_split"), 4)
                    if u >= 4:
                        pe.wait_ge(sem("hid_full"), u // 2 - 1)
                    feature_major(UP[u % 4], half, (A_W, B_W)[k], gv * P, range(3 * KT)).then_inc(sem("up"), 1)
                pe.wait_ge(sem("w_split"), 8)
                for n in range(2 * NT):
                    t, half = n // 2, n % 2
                    if n % NT == 0:
                        pe.wait_ge(sem("hid_lo"), 3 + n // NT)
                    if n >= 4:
                        pe.wait_ge(sem("down_read"), n - 3)
                    for s in range(6):
                        k, (wp, hp) = s // 3, PASSES[s % 3]
                        mm = nc.tensor.matmul(DOWN[n % 4][:], hid[hp][:, k, t * P:t * P + P],
                                              D_W[wp][:, k, half * HALF:half * HALF + HALF], start=(s == 0),
                                              stop=(s == 5))
                    mm.then_inc(sem("down"), 1)

            @block.scalar
            def _(act):
                nc.scalar.preload_act_table_set("natural_log_exp_and_others")
                for n in range(4):
                    k, half = n // 2, n % 2
                    act.wait_ge(sem("up"), 2 * n + 1)
                    if n >= 2:
                        act.wait_ge(sem("hid_lo"), n - 1)
                    nc.scalar.activation(e_buf[:, n % 2], UP[2 * n % 4][:], ACT.Exp, scale=-1.0) \
                        .then_inc(sem("gate_exp"), 1)
                    act.wait_ge(sem("hid_full"), n + 1)
                    nc.scalar.activation(hid[0][:, k, half * HALF:half * HALF + HALF], e_buf[:, n % 2], ACT.Copy) \
                        .then_inc(sem("hid_hi"), 1)
                own = Count(sem("f_act"))
                for t in range(NT if last else 0):
                    act.wait_ge(sem("down_read"), 2 * t + 2)
                    own.inc(nc.scalar.activation(f_junk[:], x1[:, t], ACT.Square, accum_out=f_ss[:, t:t + 1]))
                    own.wait(act)
                    own.inc(nc.scalar.activation(f_ss[:, t:t + 1], f_ss[:, t:t + 1], ACT.Ln, scale=1.0 / D,
                                                 bias=eps[:]))
                    own.wait(act)
                    nc.scalar.activation(f_rstd[:, t:t + 1], f_ss[:, t:t + 1], ACT.Exp, scale=-0.5) \
                        .then_inc(sem("f_rstd"), 1)

            @block.vector
            def _(dve):
                own = Count(sem("silu"))
                for n in range(4):
                    k, half = n // 2, n % 2
                    cols = slice(half * HALF, half * HALF + HALF)
                    e = e_buf[:, n % 2]
                    dve.wait_ge(sem("gate_exp"), n + 1)
                    own.inc(dve.tensor_scalar(e, e, 1.0, None, ALU.add))
                    own.wait(dve)
                    own.inc(dve.reciprocal(e, e))
                    own.wait(dve)
                    own.inc(dve.tensor_tensor(e, e, UP[2 * n % 4][:], ALU.mult))
                    own.wait(dve)
                    dve.wait_ge(sem("up"), 2 * n + 2)
                    dve.tensor_tensor(e, e, UP[2 * n % 4 + 1][:], ALU.mult).then_inc(sem("hid_full"), 1)
                    dve.wait_ge(sem("hid_full"), n + 1)
                    dve.wait_ge(sem("hid_hi"), n + 1)
                    dve.tensor_tensor(hid[1][:, k, cols], e, hid[0][:, k, cols].bitcast(F32), ALU.subtract) \
                        .then_inc(sem("hid_lo"), 1)

                def final_norm(t):
                    dve.wait_ge(sem("f_rstd"), t + 1)
                    if t == 0:
                        dve.wait_ge(sem("gain_in"), 16)
                    dve.scalar_tensor_tensor(x1[:, t], x1[:, t], f_rstd[:, t:t + 1], fin_gain[:], ALU.mult, ALU.mult) \
                        .then_inc(sem("out_ready"), 1)

                for n in range(2 * NT):
                    t, half = n // 2, n % 2
                    acc = x1[:, t, half * HALF:half * HALF + HALF]
                    dve.wait_ge(sem("down"), n + 1)
                    dve.tensor_tensor(acc, acc, DOWN[n % 4][:], ALU.add).then_inc(sem("down_read"), 1)
                    if last and half and t >= 2:
                        final_norm(t - 2)
                dve.wait_ge(sem("down_read"), 2 * NT)
                if last:
                    final_norm(NT - 2)
                    final_norm(NT - 1)
        end_section()

    with nc.Fori(0, F_STEPS - 1) as i:
        ffn_pass(i, False)
    ffn_pass(F_STEPS - 1, True)


_INS = ["x", "c", "ada_w", "ada_b", "norm_mix", "norm_ffn", "w_in", "gla_w_g2", "gla_b_g2", "gla_norm", "ml_i_bias",
        "ml_f_bias", "ml_norm", "gdn_conv", "gdn_a_log", "gdn_dt_bias", "gdn_norm", "w_out", "w_ffn_up", "w_ffn_down",
        "norm_final"]
_OUTS = [((1, S, D), "float32")]


def kernel(**inputs):
    import numpy as _np
    import concourse.bacc as _bacc
    from concourse import mybir as _mybir
    from concourse.bass_utils import run_bass_kernel_spmd as _run

    nc = _bacc.Bacc("TRN2", target_bir_lowering=False, num_devices=1)
    arrays, args = {}, []
    for name in _INS:
        a = _np.ascontiguousarray(inputs[name])
        arrays[f"in_{name}_dram"] = a
        args.append(nc.dram_tensor(f"in_{name}_dram", a.shape, _mybir.dt.from_np(a.dtype), kind="ExternalInput").ap())
    for i, (shape, dtype) in enumerate(_OUTS):
        dt = _mybir.dt.from_np(_np.dtype(dtype))
        args.append(nc.dram_tensor(f"out_{i}_dram", shape, dt, kind="ExternalOutput").ap())
    hybrid_block(nc, *args)
    r = _run(nc, [arrays], core_ids=[0])
    return r.results[0]["out_0_dram"]
```
